# Optimizing a Trainium2 kernel written in Bass

```python
import math
import jax, jax.numpy as jnp
from jax import lax
import numpy as np

D_MODEL = 1024
BATCH = 1
SEQ = 1024
DEPTH = 1
DEC_BATCH = 8
DEC_SEQ = 4
PAST_LEN = 8192
PAGE_SIZE = 128

H_A = 4
HD_A = 128
D_A = H_A * HD_A
CONV_W = 4
GDN_CHUNK = 64
H_B = 4
DH_B = 64
D_B = H_B * DH_B
SGU_CHUNK = 128
H_C = 4
N_C = 64
D_C = H_C * N_C
RANK_W = 64
RANK_A = 64
RANK_G = 128
D_MIX = D_A + D_B + D_C
AB_SPLITS = (D_A, D_A, D_A, D_A, H_A, H_A, D_B, D_B)
C_SPLITS = (D_C, D_C, D_C, RANK_W, RANK_A, RANK_G)
C_OFF = sum(AB_SPLITS)
N_C_IN = sum(C_SPLITS)
N_IN = C_OFF + N_C_IN
N_GROUPS = 4
EXPERTS_PER_GROUP = 4
N_EXPERTS = N_GROUPS * EXPERTS_PER_GROUP
TOP_K_IN_GROUP = 2
D_FF_E = 512
NORM_EPS = 1e-6
LN_EPS = 1e-5
GN_EPS = 64e-5

kernel_name = "hymba_style_gdn_sgu_rwkv7_hmoe_step"

def rmsnorm(x, w):
    x32 = x.astype(jnp.float32)
    y = x32 * lax.rsqrt(jnp.mean(x32 * x32, axis=-1, keepdims=True) + NORM_EPS)
    return (y * w.astype(jnp.float32)).astype(x.dtype)

def l2norm(x):
    return x * lax.rsqrt(jnp.sum(x * x, axis=-1, keepdims=True) + 1e-6)

def split_cols(x, sizes):
    return jnp.split(x, np.cumsum(sizes)[:-1].tolist(), axis=-1)

def causal_short_conv(x, buf, w):
    L = x.shape[1]
    xp = jnp.concatenate([buf.astype(x.dtype), x], axis=1)
    y = xp[:, 0:L] * w[0]
    for j in range(1, CONV_W):
        y = y + xp[:, j:j + L] * w[j]
    return jax.nn.silu(y), xp[:, L:]

def gated_delta_chunked(q, k, v, g, beta, s0):
    b, L, h, dk = q.shape
    dv = v.shape[-1]
    C = GDN_CHUNK
    n = -(-L // C)
    pad = n * C - L

    def blocks(t):
        t = jnp.pad(t, [(0, 0), (0, pad)] + [(0, 0)] * (t.ndim - 2))
        t = t.reshape((b, n, C) + t.shape[2:])
        return jnp.moveaxis(t, 3, 1)

    q = blocks(q) * (dk ** -0.5)
    k, v, g, beta = blocks(k), blocks(v), blocks(g), blocks(beta)
    gc = jnp.cumsum(g, axis=-1)
    idx = jnp.arange(C)
    causal = idx[:, None] >= idx[None, :]
    strict = idx[:, None] > idx[None, :]
    diff = gc[..., :, None] - gc[..., None, :]
    decay = jnp.where(causal, jnp.exp(jnp.where(causal, diff, 0.0)), 0.0)
    k_beta = k * beta[..., None]
    lower = jnp.where(strict, jnp.einsum('bhnid,bhnjd->bhnij', k_beta, k) * decay, 0.0)
    eye = jnp.eye(C, dtype=q.dtype)
    rhs = jnp.concatenate([v * beta[..., None], k_beta * jnp.exp(gc)[..., None]], axis=-1)
    sol = lax.linalg.triangular_solve(eye + lower, rhs, left_side=True, lower=True,
                                      unit_diagonal=True)
    u, w = sol[..., :dv], sol[..., dv:]
    attn = jnp.einsum('bhnid,bhnjd->bhnij', q, k) * decay
    q_dec = q * jnp.exp(gc)[..., None]
    k_dec = k * jnp.exp(gc[..., -1:] - gc)[..., None]
    g_last = jnp.exp(gc[..., -1])
    xs = tuple(jnp.moveaxis(t, 2, 0) for t in (u, w, attn, q_dec, k_dec, g_last))

    def step(s, inp):
        u_n, w_n, a_n, qd_n, kd_n, gl_n = inp
        v_new = u_n - jnp.einsum('bhck,bhkv->bhcv', w_n, s)
        o_n = jnp.einsum('bhck,bhkv->bhcv', qd_n, s) + jnp.einsum('bhij,bhjv->bhiv', a_n, v_new)
        s = s * gl_n[..., None, None] + jnp.einsum('bhck,bhcv->bhkv', kd_n, v_new)
        return s, o_n

    s_final, o = lax.scan(step, s0, xs)
    o = jnp.transpose(o, (1, 0, 3, 2, 4)).reshape(b, n * C, h, dv)[:, :L]
    return o, s_final

def rwkv7_recurrence(r, w, k, v, kk, a, s0):
    def step(s, inp):
        r_t, w_t, k_t, v_t, kk_t, a_t = inp
        sk = jnp.einsum('bhvk,bhk->bhv', s, kk_t)
        s = (s * w_t[:, :, None, :] - sk[..., None] * (kk_t * a_t)[:, :, None, :]
             + v_t[..., None] * k_t[:, :, None, :])
        return s, jnp.einsum('bhvk,bhk->bhv', s, r_t)

    xs = tuple(jnp.moveaxis(t, 1, 0) for t in (r, w, k, v, kk, a))
    s, y = lax.scan(step, s0, xs)
    return jnp.moveaxis(y, 0, 1), s

def sgu_mix(v, w_s, b_s):
    b, L, hh, d = v.shape
    n = -(-L // SGU_CHUNK)
    vp = jnp.pad(v, ((0, 0), (0, n * SGU_CHUNK - L), (0, 0), (0, 0))).reshape(b, n, SGU_CHUNK, hh, d)
    t = jnp.arange(SGU_CHUNK)
    wm = jnp.where(t[:, None] >= t[None, :], w_s.astype(jnp.float32), 0.0)
    out = jnp.einsum('hts,bnshd->bnthd', wm, vp) + jnp.transpose(b_s.astype(jnp.float32))[:, :, None]
    return out.reshape(b, n * SGU_CHUNK, hh, d)[:, :L]

def token_mixers(h, p, s_gdn, conv_buf, s_rwkv, h_prev):
    f32 = jnp.float32
    b, L, _ = h.shape
    proj = h @ p['w_in']
    qa, ka, va, za, ba, aa, ub, vb = split_cols(proj[..., :C_OFF], AB_SPLITS)

    qkv, new_conv = causal_short_conv(jnp.concatenate([qa, ka, va], axis=-1), conv_buf, p['gdn_conv_w'])
    q, k, v = (t.astype(f32).reshape(b, L, H_A, HD_A) for t in jnp.split(qkv, 3, axis=-1))
    q, k = l2norm(q), l2norm(k)
    beta = jax.nn.sigmoid(ba.astype(f32))
    g = -jnp.exp(p['gdn_a_log'].astype(f32)) * jax.nn.softplus(aa.astype(f32) + p['gdn_dt_bias'].astype(f32))
    o, new_gdn = gated_delta_chunked(q, k, v, g, beta, s_gdn.astype(f32))
    o = o * lax.rsqrt(jnp.mean(o * o, axis=-1, keepdims=True) + NORM_EPS) * p['gdn_norm_w'].astype(f32)
    o_a = (o * jax.nn.silu(za.astype(f32).reshape(b, L, H_A, HD_A))).reshape(b, L, D_A)

    u = jax.nn.gelu(ub.astype(f32), approximate=False)
    vs = jax.nn.gelu(vb.astype(f32), approximate=False).reshape(b, L, H_B, DH_B)
    mu_v = jnp.mean(vs, axis=-1, keepdims=True)
    var_v = jnp.mean(jnp.square(vs - mu_v), axis=-1, keepdims=True)
    vs = ((vs - mu_v) * lax.rsqrt(var_v + LN_EPS) * p['sgu_ln_w'].astype(f32).reshape(H_B, DH_B)
          + p['sgu_ln_b'].astype(f32).reshape(H_B, DH_B))
    o_b = u * sgu_mix(vs, p['sgu_w'], p['sgu_b']).reshape(b, L, D_B)

    pc = proj[..., C_OFF:]
    pc_first = (h_prev.astype(h.dtype) @ p['w_in'][:, C_OFF:])[:, None]
    p_prev = jnp.concatenate([pc_first, pc[:, :-1]], axis=1)
    pm = (pc + p['rwkv_mu'] * (p_prev - pc)).astype(f32)
    r, kc, vc, wd, ad, gd = split_cols(pm, C_SPLITS)
    w_log = -jax.nn.softplus(-(p['rwkv_w0'] + jnp.tanh(wd) @ p['rwkv_w_up'])) - 0.5
    decay = jnp.exp(-jnp.exp(w_log))
    a = jax.nn.sigmoid(p['rwkv_a0'] + ad @ p['rwkv_a_up'])
    gate = jax.nn.sigmoid(gd) @ p['rwkv_g_up']
    heads = lambda t: t.reshape(b, L, H_C, N_C)
    kk = l2norm(heads(kc * p['rwkv_k_k']))
    kc = kc * (1.0 + (a - 1.0) * p['rwkv_k_a'])
    r, kc, vc, a, decay = (heads(t.astype(f32)) for t in (r, kc, vc, a, decay))
    y, new_rwkv = rwkv7_recurrence(r, decay, kc, vc, kk, a, s_rwkv.astype(f32))
    mu_y = jnp.mean(y, axis=-1, keepdims=True)
    var_y = jnp.mean(jnp.square(y - mu_y), axis=-1, keepdims=True)
    y = ((y - mu_y) * lax.rsqrt(var_y + GN_EPS) * p['rwkv_ln_w'].astype(f32).reshape(H_C, N_C)
         + p['rwkv_ln_b'].astype(f32).reshape(H_C, N_C))
    bonus = jnp.sum(r * kc * p['rwkv_r_k'].astype(f32), axis=-1, keepdims=True) * vc
    o_c = (y + bonus).reshape(b, L, D_C) * gate

    mix = jnp.concatenate([o_a, o_b, o_c], axis=-1).astype(h.dtype) @ p['w_out']
    return mix, new_gdn, new_conv, new_rwkv, h[:, -1], vs.reshape(b, L, D_B)

def hier_moe(h, p):
    f32 = jnp.float32
    b, L, _ = h.shape
    gl = (h @ p['router_group_w']).astype(f32) + p['router_group_b'].astype(f32)
    gsel = jnp.argmax(gl, axis=-1)
    gw = jnp.take_along_axis(jax.nn.softmax(gl, axis=-1), gsel[..., None], axis=-1)
    el = ((h @ p['router_expert_w']).astype(f32) + p['router_expert_b'].astype(f32)).reshape(
        b, L, N_GROUPS, EXPERTS_PER_GROUP)
    el_sel = jnp.take_along_axis(el, gsel[..., None, None], axis=2)[..., 0, :]
    top_v, top_i = lax.top_k(el_sel, TOP_K_IN_GROUP)
    tw = jax.nn.softmax(top_v, axis=-1) * gw
    eid = gsel[..., None] * EXPERTS_PER_GROUP + top_i
    gate = jnp.sum(jax.nn.one_hot(eid, N_EXPERTS, dtype=f32) * tw[..., None], axis=-2)
    y = jnp.zeros(h.shape, f32)
    for e in range(N_EXPERTS):
        he = jax.nn.silu(h @ p['expert_w_gate'][e]) * (h @ p['expert_w_up'][e])
        y = y + gate[..., e:e + 1] * (he @ p['expert_w_down'][e]).astype(f32)
    return y.astype(h.dtype)

def forward_group(x, s_gdn, conv_buf, s_rwkv, h_prev, layers, norm_final, keep_chunk_rows):
    new = ([], [], [], [], [])
    for l in range(DEPTH):
        p = layers[l]
        mix, n_gdn, n_conv, n_rwkv, n_shift, v_rows = token_mixers(
            rmsnorm(x, p['norm_mix']), p, s_gdn[l], conv_buf[l], s_rwkv[l], h_prev[l])
        x = x + mix.astype(x.dtype)
        x = x + hier_moe(rmsnorm(x, p['norm_ffn']), p)
        new[0].append(n_gdn)
        new[1].append(n_conv)
        new[2].append(n_rwkv)
        new[3].append(n_shift)
        if keep_chunk_rows:
            new[4].append(v_rows)
    return rmsnorm(x, norm_final), new

def setup_inputs(seed: int = 0) -> dict:
    key = jax.random.key(seed)
    keys = iter(jax.random.split(key, 64))
    f32 = jnp.float32

    def nrm(shape, scale):
        return scale * jax.random.normal(next(keys), shape, f32)

    def unif(shape, lo, hi):
        return jax.random.uniform(next(keys), shape, f32, lo, hi)

    dt = jnp.exp(unif((DEPTH, H_A), math.log(1e-3), math.log(1e-1)))
    return {
        'x_prompt': nrm((BATCH, SEQ, D_MODEL), 1.0),
        'x_sample': nrm((DEC_BATCH, DEC_SEQ, D_MODEL), 1.0),
        'state_gdn': nrm((DEPTH, DEC_BATCH, H_A, HD_A, HD_A), 0.3),
        'state_gdn_conv': nrm((DEPTH, DEC_BATCH, CONV_W - 1, 3 * D_A), 1.0),
        'state_rwkv': nrm((DEPTH, DEC_BATCH, H_C, N_C, N_C), 0.5),
        'state_rwkv_shift': nrm((DEPTH, DEC_BATCH, D_MODEL), 1.0),
        'norm_mix': 1.0 + nrm((DEPTH, D_MODEL), 0.02),
        'norm_ffn': 1.0 + nrm((DEPTH, D_MODEL), 0.02),
        'norm_final': 1.0 + nrm((D_MODEL,), 0.02),
        'w_in': nrm((DEPTH, D_MODEL, N_IN), D_MODEL ** -0.5),
        'gdn_conv_w': nrm((DEPTH, CONV_W, 3 * D_A), CONV_W ** -0.5),
        'gdn_a_log': jnp.log(unif((DEPTH, H_A), 1.0, 16.0)),
        'gdn_dt_bias': jnp.log(jnp.expm1(dt)),
        'gdn_norm_w': 1.0 + nrm((DEPTH, HD_A), 0.02),
        'sgu_ln_w': 1.0 + nrm((DEPTH, D_B), 0.02),
        'sgu_ln_b': nrm((DEPTH, D_B), 0.02),
        'sgu_w': nrm((DEPTH, H_B, SGU_CHUNK, SGU_CHUNK), SGU_CHUNK ** -0.5),
        'sgu_b': 1.0 + nrm((DEPTH, H_B, SGU_CHUNK), 0.02),
        'rwkv_mu': unif((DEPTH, N_C_IN), 0.0, 1.0),
        'rwkv_w0': unif((DEPTH, D_C), -6.0, -1.0),
        'rwkv_w_up': nrm((DEPTH, RANK_W, D_C), 0.1),
        'rwkv_a0': nrm((DEPTH, D_C), 0.1),
        'rwkv_a_up': nrm((DEPTH, RANK_A, D_C), RANK_A ** -0.5),
        'rwkv_g_up': nrm((DEPTH, RANK_G, D_C), RANK_G ** -0.5),
        'rwkv_k_k': 0.85 + nrm((DEPTH, D_C), 0.05),
        'rwkv_k_a': 1.0 + nrm((DEPTH, D_C), 0.05),
        'rwkv_r_k': nrm((DEPTH, H_C, N_C), 0.1),
        'rwkv_ln_w': 1.0 + nrm((DEPTH, D_C), 0.02),
        'rwkv_ln_b': nrm((DEPTH, D_C), 0.02),
        'w_out': nrm((DEPTH, D_MIX, D_MODEL), D_MIX ** -0.5),
        'router_group_w': nrm((DEPTH, D_MODEL, N_GROUPS), D_MODEL ** -0.5),
        'router_group_b': nrm((DEPTH, N_GROUPS), 0.01),
        'router_expert_w': nrm((DEPTH, D_MODEL, N_EXPERTS), D_MODEL ** -0.5),
        'router_expert_b': nrm((DEPTH, N_EXPERTS), 0.01),
        'expert_w_gate': nrm((DEPTH, N_EXPERTS, D_MODEL, D_FF_E), D_MODEL ** -0.5),
        'expert_w_up': nrm((DEPTH, N_EXPERTS, D_MODEL, D_FF_E), D_MODEL ** -0.5),
        'expert_w_down': nrm((DEPTH, N_EXPERTS, D_FF_E, D_MODEL), D_FF_E ** -0.5),
    }

def reference(x_prompt, x_sample, state_gdn, state_gdn_conv, state_rwkv, state_rwkv_shift,
              norm_mix, norm_ffn, norm_final, w_in, gdn_conv_w, gdn_a_log, gdn_dt_bias, gdn_norm_w,
              sgu_ln_w, sgu_ln_b, sgu_w, sgu_b, rwkv_mu, rwkv_w0, rwkv_w_up, rwkv_a0, rwkv_a_up,
              rwkv_g_up, rwkv_k_k, rwkv_k_a, rwkv_r_k, rwkv_ln_w, rwkv_ln_b, w_out,
              router_group_w, router_group_b, router_expert_w, router_expert_b,
              expert_w_gate, expert_w_up, expert_w_down):
    stacked = dict(norm_mix=norm_mix, norm_ffn=norm_ffn, w_in=w_in, gdn_conv_w=gdn_conv_w,
                   gdn_a_log=gdn_a_log, gdn_dt_bias=gdn_dt_bias, gdn_norm_w=gdn_norm_w,
                   sgu_ln_w=sgu_ln_w, sgu_ln_b=sgu_ln_b, sgu_w=sgu_w, sgu_b=sgu_b,
                   rwkv_mu=rwkv_mu, rwkv_w0=rwkv_w0, rwkv_w_up=rwkv_w_up, rwkv_a0=rwkv_a0,
                   rwkv_a_up=rwkv_a_up, rwkv_g_up=rwkv_g_up, rwkv_k_k=rwkv_k_k, rwkv_k_a=rwkv_k_a,
                   rwkv_r_k=rwkv_r_k, rwkv_ln_w=rwkv_ln_w, rwkv_ln_b=rwkv_ln_b, w_out=w_out,
                   router_group_w=router_group_w, router_group_b=router_group_b,
                   router_expert_w=router_expert_w, router_expert_b=router_expert_b,
                   expert_w_gate=expert_w_gate, expert_w_up=expert_w_up, expert_w_down=expert_w_down)
    layers = [{name: arr[l] for name, arr in stacked.items()} for l in range(DEPTH)]
    b = x_prompt.shape[0]
    z_gdn = jnp.zeros((DEPTH, b, H_A, HD_A, HD_A), state_gdn.dtype)
    z_conv = jnp.zeros((DEPTH, b, CONV_W - 1, 3 * D_A), x_prompt.dtype)
    z_rwkv = jnp.zeros((DEPTH, b, H_C, N_C, N_C), state_rwkv.dtype)
    z_shift = jnp.zeros((DEPTH, b, D_MODEL), x_prompt.dtype)
    y_prompt, np_ = forward_group(x_prompt, z_gdn, z_conv, z_rwkv, z_shift, layers, norm_final, False)
    y_sample, ns_ = forward_group(x_sample, state_gdn, state_gdn_conv, state_rwkv, state_rwkv_shift,
                                  layers, norm_final, True)
    gdn_p = jnp.stack(np_[0]).astype(state_gdn.dtype)
    conv_p = jnp.stack(np_[1]).astype(state_gdn_conv.dtype)
    rwkv_p = jnp.stack(np_[2]).astype(state_rwkv.dtype)
    shift_p = jnp.stack(np_[3]).astype(state_rwkv_shift.dtype)
    gdn_s = jnp.stack(ns_[0]).astype(state_gdn.dtype)
    conv_s = jnp.stack(ns_[1]).astype(state_gdn_conv.dtype)
    rwkv_s = jnp.stack(ns_[2]).astype(state_rwkv.dtype)
    shift_s = jnp.stack(ns_[3]).astype(state_rwkv_shift.dtype)
    chunk_v_s = jnp.stack(ns_[4]).astype(x_sample.dtype)
    return (y_prompt, y_sample, gdn_p, conv_p, rwkv_p, shift_p, gdn_s, conv_s, rwkv_s, shift_s, chunk_v_s)


_drawn_inputs = setup_inputs


def setup_inputs(seed=0):
    import zlib

    import numpy as np

    out = dict(_drawn_inputs(seed))
    spreads = {}
    factors = {'norm_final': 8.178,
     'sgu_ln_w': 8.72,
     'sgu_ln_b': 8.959,
     'sgu_b': 21.484,
     'rwkv_ln_w': 22.6,
     'rwkv_ln_b': 21.17,
     'router_expert_b': 25.979,
     'norm_ffn': 6.74,
     'gdn_norm_w': 8.0,
     'router_group_b': 7.219}
    for name, (base, spread) in spreads.items():
        noise = np.random.default_rng([zlib.crc32(name.encode()), seed]).standard_normal(out[name].shape)
        drawn = base * np.exp(spread * noise) if base else spread * noise
        out[name] = __import__('jax').numpy.asarray(drawn.astype(out[name].dtype))
    for name, factor in factors.items():
        out[name] = (out[name] * factor).astype(out[name].dtype)
    return out
```

```python
from contextlib import ExitStack
import math

import numpy as np

import concourse.bass as bass
from concourse import mybir

ds = bass.ds
F32 = mybir.dt.float32
U32 = mybir.dt.uint32
I32 = mybir.dt.int32
ALU = mybir.AluOpType
ACT = mybir.ActivationFunctionType
AX_X = mybir.AxisListType.X

P = 128
D = 1024
KD = D // P
SEQ = 1024
NT = SEQ // P
NB, TB = 8, 4
NS = NB * TB
NTOK = SEQ + NS
NEXT = NTOK + NB
TILES = NT + 1
CH = 352
H = 4
HA = 128
HC = 64
CW = 4
DA, DB, DC = H * HA, H * HC, H * HC
NIN = 4 * DA + 2 * H + 2 * DB + 3 * DC + 64 + 64 + 128
COL_GATE = 4 * DA
COL_U = COL_GATE + 2 * H
COL_C = COL_U + 2 * DB
NORM_EPS, LN_EPS, GN_EPS, L2_EPS = 1e-6, 1e-5, 64e-5, 1e-6
LNEXP = "natural_log_exp_and_others"
DECAY = -math.exp(-0.5)

ROWS = {}
_at = 0
for _n, _r in (("norm_mix", 8), ("norm_ffn", 8), ("gdn_conv_w", 48), ("rwkv_mu", 8), ("rwkv_w0", 2), ("rwkv_a0", 2),
               ("rwkv_k_k", 2), ("rwkv_k_a", 2), ("rwkv_r_k", 2), ("rwkv_ln_w", 2), ("rwkv_ln_b", 2),
               ("gdn_norm_w", 1)):
    ROWS[_n] = (_at, _r)
    _at += _r
NROWS = _at

SEMS = """masks zeroed rows setupT cs sw small samp_w
x0 x1 rstd hn xT hT shift_out
w0 w1 pj pj_evac conv silu mixd sq nrm nrm_ln rs nrm_done gt_sb gt_T gt_ready
gb g_e tails tails_sb out_c drv""".split()
SGU_SEMS = "vT var rstd vn mix vout rows_out".split()
OUT_SEMS = "w x mixT out x2 rstd h2 h2p h2T h2o sent lg lgs wr rt ex".split()
MOE_SEMS = "w0 w1 gather xTp xT gu silu he down acc yout done zero fill filled".split()
FIN_SEMS = "w c0 c1 c2 used rstd y out".split()
SLOTS = 32
NE, NG, EPG, FF = 16, 4, 4, 512


def tokens(t):
    return t * P


class Names(dict):
    __getattr__ = dict.__getitem__


class Ctx:

    def __init__(self, nc, stack):
        self.nc, self.stack = nc, stack

    def sb(self, name, *shape, dt=F32):
        return self.stack.enter_context(self.nc.sbuf_tensor(name, list(shape), dt))


def bc(ap, axis, n):
    u = ap.unsqueeze(axis)
    shape = list(u.shape)
    shape[axis] = n
    return u.to_broadcast(shape)


def make_masks(pool, m, s):
    g = pool
    for a, v in ((m.ident, 0.0), (m.ones, 1.0), (m.causal, 1.0), (m.blk64, 1.0), (m.rw, 1.0), (m.lev, 0.0),
                 (m.causal4, 1.0), (m.rw4, 1.0), (m.blk4, 1.0), (m.seq4, 1.0), (m.reset, 1.0), (m.sguS, 0.0),
                 (m.reset4, 1.0)):
        g.memset(a[:], v)
    g.drain()

    def sel(view, pattern, base, chm, op=ALU.is_ge, fill=0.0):
        g.affine_select(out=view, in_=view, compare_op=op, fill=fill, base=base, pattern=pattern,
                        channel_multiplier=chm)
        g.drain()

    sel(m.ident[:], [[-1, P]], 0, 1, ALU.not_equal, 1.0)
    sel(m.causal[:], [[1, P]], 0, -1)
    v = m.blk64[:].rearrange("p (b n) -> p b n", b=2)
    sel(v, [[-64, 2], [0, 64]], 0, 1)
    sel(v, [[64, 2], [0, 64]], 63, -1)
    for x in range(2):
        v = m.rw[:, x, :].rearrange("p (b n) -> p b n", b=2)
        sel(v, [[-64, 2], [0, 64]], 0, 1)
        sel(v, [[64, 2], [1, 64]], x - 1, -1)
        v = m.rw4[:, x, :].rearrange("p (b n) -> p b n", b=NB)
        sel(v, [[-TB, NB], [0, TB]], 0, 1)
        sel(v, [[TB, NB], [1, TB]], x - 1, -1)
    v = m.causal4[:].rearrange("p (b n) -> p b n", b=NB)
    sel(v, [[-TB, NB], [0, TB]], 0, 1)
    sel(v, [[TB, NB], [1, TB]], 0, -1)
    v = m.blk4[:].rearrange("p (b n) -> p b n", b=NB)
    sel(v, [[-TB, NB], [0, TB]], 0, 1)
    sel(v, [[TB, NB], [0, TB]], TB - 1, -1)
    sel(m.seq4[:], [[-TB, NB]], 0, 1)
    sel(m.seq4[:], [[TB, NB]], TB - 1, -1)
    g.memset(m.reset[:].rearrange("p (b n) -> p b n", n=64)[:, :, 0:1], 0.0)
    g.memset(m.reset4[:].rearrange("p (b n) -> p b n", n=TB)[:, :, 0:1], 0.0)
    for k in range(7):
        h = 1 << k
        nb = P // (2 * h)
        v = m.lev[:, k, :].rearrange("p (b x n) -> p b x n", x=2, n=h)[:, :, 1, :]
        g.memset(v, 1.0)
        g.drain()
        sel(v, [[-2 * h, nb], [0, h]], 0, 1)
        sel(v, [[2 * h, nb], [0, h]], h - 1, -1)
    g.nop().then_inc(s.masks, 1)


def build(nc, A, O, debug=None):
    with ExitStack() as root:
        root.enter_context(nc.allow_non_contiguous_dma(reason="small transposed parameters and state rows"))

        def sems(prefix, names):
            return Names(**{n: root.enter_context(nc.semaphore(prefix + n)) for n in names})

        s = sems("s_", SEMS)
        ps = root.enter_context(nc.psum_tensor("ps", [P, 8, 512], F32))
        C = Ctx(nc, root)
        m = Names()
        m.ident, m.ones, m.causal, m.blk64 = (C.sb(n, P, P) for n in ("ident", "ones", "causal", "blk64"))
        m.rw, m.lev = C.sb("rw_mask", P, 2, P), C.sb("lev_mask", P, 7, P)
        m.causal4, m.rw4, m.blk4, m.seq4 = C.sb("causal4", NS, NS), C.sb("rw4_mask", NS, 2, NS), C.sb("blk4", NS, NS), C.sb("seq4", NS, NB)
        m.reset, m.reset4 = C.sb("reset", P, P), C.sb("reset4", P, NS)
        vecs = C.sb("vecs", P, NROWS)
        m.omka = C.sb("one_minus_ka", P, 2)
        lora = C.sb("lora_up", P, DC)
        gup = C.sb("g_up", P, DC)
        gts = C.sb("gate_scales", P, 2, H)
        g_all = C.sb("g_all", P, TILES, H)
        beta_all = C.sb("beta_all", P, TILES, H)
        gcum = C.sb("gcum", P, TILES, H)
        kdf = C.sb("k_dec_factor", P, TILES, H)
        gl_all = C.sb("chunk_decay", P, TILES, H)
        glS = C.sb("chunk_decay_sample", P, NB, H)
        persist = root.enter_context(ExitStack())
        Q = Ctx(nc, persist)
        qkv = Q.sb("qkv", P, 12, NTOK)
        zg = Q.sb("zg", P, 4, NTOK)
        ub = Q.sb("ub", P, 2, NTOK)
        cb = Q.sb("cb", P, 8, NTOK)
        lw = Q.sb("lw", P, 2, NTOK)
        bb = Q.sb("bb", P, 2, NTOK)

        def vec(name, i=0, n=1):
            a = ROWS[name][0] + i
            return vecs[:, a:a + n]

        pre = [Q.sb(f"pre_{u}", P, 3 + SEQ + NB * (3 + TB)) for u in range(2)]
        kk = [pre[c][:, 0:NTOK] for c in range(2)]
        v_stack = root.enter_context(ExitStack())
        G = Ctx(nc, v_stack)
        vbn = G.sb("vbn", P, 2, NTOK)
        m.sguS = G.sb("sgu_wT_sample", NS, H, NS)
        sguT = G.sb("sgu_wT", P, H, P)
        sgb = G.sb("sgu_bias", P, 2, P)
        lnwb = G.sb("sgu_ln", P, 2, DB)
        p1 = root.enter_context(ExitStack())
        T = Ctx(nc, p1)
        hT = T.sb("hT", P, KD, NEXT)
        wbuf = [T.sb(f"w_in_{u}", P, KD, P) for u in range(2)]
        wg = T.sb("w_gate_cols", P, KD, 2 * H)
        cst = T.sb("conv_state_T", P, 12, NB * 3)
        tails = T.sb("conv_tails", P, 12, 3 + NB * 3)

        with nc.Block() as block:
            stage = qkv[:].rearrange("p a n -> p (a n)")
            rowtab = stage[0:NROWS, 0:P]
            sguw = stage[:, 128:640].rearrange("p (h n) -> p h n", h=H)
            cs_in = stage[0:NB * 3, 640:640 + 3 * DA]
            hp_in = stage[0:NB, 2176:2176 + D]
            x = [stage[:, 3200 + u * D:3200 + (u + 1) * D] for u in range(2)]
            hn = [stage[:, 5248 + u * D:5248 + (u + 1) * D] for u in range(2)]
            junk = stage[:, 7296:7296 + D]
            ssq = [stage[:, 8320 + 8 * u:8322 + 8 * u] for u in range(2)]
            nrow_dmas = len(ROWS)
            x_in = (s.x0, s.x1)

            @block.gpsimd
            def _(pool):
                make_masks(pool, m, s)
                pool.wait_ge(s.samp_w, 16 * NB * H)
                pool.tensor_tensor(m.sguS[:], m.sguS[:], bc(m.causal4[:], 1, H), ALU.mult)

            @block.sync
            def _(sp):
                for n, (r0, r) in ROWS.items():
                    src = A[n]
                    if n == "gdn_conv_w":
                        src = src.rearrange("o j (b p) -> (o j b) p", p=P)
                    elif n == "rwkv_r_k":
                        src = src.rearrange("o (r a) n -> (o r) (a n)", a=2)
                    else:
                        src = src.rearrange("o (r p) -> (o r) p", p=P)
                    sp.dma_start(rowtab[r0:r0 + r, :], src).then_inc(s.rows, 16)

                def load_x(i, u, rows, src):
                    T_ = 2 * i + u
                    sp.wait_ge(s.hn, T_ + 1)
                    sp.dma_start(x[u][0:rows, :], src).then_inc(x_in[u], 16)

                sp.dma_start(cs_in, A["state_gdn_conv"].rearrange("o b j c -> (o b j) c")).then_inc(s.cs, 16)
                sp.dma_start(hp_in, A["state_rwkv_shift"][0]).then_inc(s.cs, 16)
                with sp.Fori(0, NT // 2) as i:
                    for u in range(2):
                        load_x(i, u, P, A["x_prompt"][0, ds((2 * i + u) * P, P), :])
                load_x(NT // 2, 0, NS, A["x_sample"].rearrange("b t d -> (b t) d"))
                sp.dma_start(sguw, A["sgu_w"][0].rearrange("h t s -> t h s")).then_inc(s.sw, 16)
                for i, (dst, src) in enumerate((
                        (lora[0:64, :], A["rwkv_w_up"][0]), (lora[64:128, :], A["rwkv_a_up"][0]), (gup[:], A["rwkv_g_up"][0]),
                        (gts[:, 0, :], A["gdn_a_log"][0].partition_broadcast(P)),
                        (gts[:, 1, :], A["gdn_dt_bias"][0].partition_broadcast(P)),
                        (lnwb[:, 0, :], A["sgu_ln_w"][0].partition_broadcast(P)),
                        (lnwb[:, 1, :], A["sgu_ln_b"][0].partition_broadcast(P)),
                        (sgb[0:64, :, :], A["sgu_b"][0].rearrange("(c x) t -> x c t", x=2)[0].partition_broadcast(64)),
                        (sgb[64:128, :, :], A["sgu_b"][0].rearrange("(c x) t -> x c t", x=2)[1].partition_broadcast(64)),
                        (wg[:], A["w_in"][0, :, COL_GATE:COL_U].rearrange("(k p) c -> p k c", p=P)))):
                    sp.dma_start(dst, src).then_inc(s.small, 16)
                sp.wait_ge(s.masks, 1)
                for b in range(NB):
                    for h in range(H):
                        sp.dma_start(m.sguS[TB * b:TB * b + TB, h, TB * b:TB * b + TB],
                                     A["sgu_w"][0, h, 0:TB, 0:TB].rearrange("t s -> s t")).then_inc(s.samp_w, 16)
                sp.wait_ge(s.small, 16 * 10)

            @block.tensor
            def _(pe):
                pe.wait_ge(s.masks, 1)
                pe.wait_ge(s.rows, 16 * nrow_dmas)
                pe.transpose(ps[:, 4, 0:NROWS], rowtab, m.ident[0:NROWS, 0:NROWS]).then_inc(s.setupT, 1)
                pe.wait_ge(s.cs, 32)
                for b in range(12):
                    last = pe.transpose(ps[:, 5, 24 * b:24 * b + 24], cs_in[:, b * P:b * P + P], m.ident[0:24, 0:24])
                last.then_inc(s.setupT, 1)
                for k in range(KD):
                    last = pe.transpose(ps[:, 6, NB * k:NB * k + NB], hp_in[:, k * P:k * P + P], m.ident[0:NB, 0:NB])
                last.then_inc(s.setupT, 1)

                def token_tile(i, u, n):
                    T_ = 2 * i + u
                    pe.wait_ge(s.hn, T_ + 3)
                    pe.wait_ge(s.hT, T_ + 1)
                    for k in range(KD):
                        last = pe.transpose(ps[:, 2 * u + k // 4, (k % 4) * P:(k % 4) * P + n], hn[u][0:n, k * P:k * P + P],
                                            m.ident[0:n, 0:n])
                    last.then_inc(s.xT, 1)

                with pe.Fori(0, NT // 2) as i:
                    for u in range(2):
                        token_tile(i, u, P)
                token_tile(NT // 2, 0, NS)
                pe.wait_ge(s.sw, 16)
                for h in range(H):
                    last = pe.transpose(ps[:, 7, h * P:h * P + P], sguw[:, h, :], m.ident[:])
                last.then_inc(s.setupT, 1)

            @block.scalar
            def _(act):
                act.preload_act_table_set(LNEXP)

                def stats(i, u, n):
                    T_ = 2 * i + u
                    act.wait_ge(x_in[u], 16 * (i + 1))
                    act.wait_ge(s.hn, T_ + 1)
                    act.activation(junk[0:n, :], x[u][0:n, :], ACT.Square, accum_out=ssq[u][0:n, 0:1])
                    act.drain()
                    act.activation(ssq[u][0:n, 1:2], ssq[u][0:n, 0:1], ACT.Ln, scale=1.0 / D, bias=NORM_EPS)
                    act.drain()
                    act.activation(ssq[u][0:n, 0:1], ssq[u][0:n, 1:2], ACT.Exp, scale=-0.5).then_inc(s.rstd, 1)

                with act.Fori(0, NT // 2) as i:
                    for u in range(2):
                        stats(i, u, P)
                stats(NT // 2, 0, NS)

            @block.vector
            def _(dve):
                dve.sem_inc(s.hn, 2)
                dve.sem_inc(s.hT, 2)
                dve.sem_inc(s.xT, 2)
                dve.wait_ge(s.setupT, 1)
                dve.tensor_copy(vecs[:], ps[:, 4, 0:NROWS])
                dve.drain()
                dve.tensor_scalar(m.omka[:], vec("rwkv_k_a", 0, 2), -1.0, 1.0, ALU.mult, ALU.add)
                dve.wait_ge(s.setupT, 2)
                dve.tensor_copy(cst[:].rearrange("p a b -> p (a b)"), ps[:, 5, 0:12 * 24])
                dve.wait_ge(s.setupT, 3)
                dve.tensor_copy(hT[:, :, NTOK:NEXT], ps[:, 6, 0:KD * NB].rearrange("p (k b) -> p k b", b=NB))

                def norm(i, u, n, col):
                    T_ = 2 * i + u
                    dve.wait_ge(s.rstd, T_ + 1)
                    dve.wait_ge(s.xT, T_ + 1)
                    dve.tensor_scalar(hn[u][0:n, :], x[u][0:n, :], ssq[u][0:n, 0:1], None, ALU.mult).then_inc(s.hn, 1)
                    dve.wait_ge(s.xT, T_ + 3)
                    dve.tensor_tensor(hT[:, :, col], ps[:, 2 * u:2 * u + 2, :].rearrange("p a (k n) -> p (a k) n", n=P)[:, :, 0:n],
                                      bc(vec("norm_mix", 0, KD), 2, n), ALU.mult).then_inc(s.hT, 1)

                with dve.Fori(0, NT // 2) as i:
                    for u in range(2):
                        norm(i, u, P, ds((2 * i + u) * P, P))
                norm(NT // 2, 0, NS, slice(SEQ, NTOK))
                dve.wait_ge(s.setupT, 4)
                dve.tensor_tensor(sguT[:], ps[:, 7, :].rearrange("p (h t) -> p h t", h=H), bc(m.causal[:], 1, H), ALU.mult)

        pst = root.enter_context(ExitStack())
        W = Ctx(nc, pst)
        acc2 = zg[:, 2:4, :]
        acc = [acc2[:, u, :] for u in range(2)]
        sq, rs, dtmp = acc[0], acc[1], lw[:, 0, :]
        XB = 3 + SEQ

        def smp(buf, off, w, lo, hi):
            return buf[:, off:off + NB * w].rearrange("p (b t) -> p b t", t=w)[:, :, lo:hi]

        def pbank(u):
            return ps[:, 3 * u:3 * u + 3, :]

        NPQ, NPC, NPZ = 12, 8, 8
        tails_rows = acc2.rearrange("p a n -> p (a n)")[0:3 + NB * 3, 0:3 * DA]
        gt8 = ub[0:2 * H, 0, :]
        GATE_BLK = NPQ + NPC
        LORA_BLK = GATE_BLK + 1
        TAIL_BLK = LORA_BLK + 6
        Z_BLK = TAIL_BLK + 1
        gtk = W.sb("gates_tokens", P, TILES, 2 * H)
        gtmp = W.sb("gates_tmp", P, 4, TILES, H)
        gsel = W.sb("g_by_sequence", NS, NB, H)

        with nc.Block() as block:
            @block.sync
            def _(sp):
                it = 0
                for n_it, base in ((NPQ // 2, 0), (NPC // 2, COL_C)):
                    with sp.Fori(0, n_it) as i:
                        for u in range(2):
                            sp.wait_ge(s.pj, 2 * (i + it) + u + 1)
                            sp.dma_start(wbuf[u][:], A["w_in"][0, :, ds(base + (2 * i + u) * P, P)].rearrange("(k p) c -> p k c", p=P))\
                                .then_inc((s.w0, s.w1)[u], 16)
                    it += n_it
                for j in range(NPZ):
                    col = 3 * DA + j * P if j < 4 else COL_U + (j - 4) * P
                    sp.wait_ge(s.pj, (GATE_BLK if j < 2 else Z_BLK) + j + 1)
                    sp.dma_start(wbuf[j % 2][:], A["w_in"][0, :, col:col + P].rearrange("(k p) c -> p k c", p=P))\
                        .then_inc((s.w0, s.w1)[j % 2], 16)

            @block.gpsimd
            def _(pool):
                pool.dma_start(O["shift_prompt"].rearrange("o b (k p) -> p (o b k)", p=P), hT[:, :, SEQ - 1]).then_inc(s.shift_out, 16)
                for b in range(NB):
                    pool.dma_start(O["shift_sample"][0, b].rearrange("(k p) -> p k", p=P),
                                 hT[:, :, SEQ + TB * b + TB - 1]).then_inc(s.shift_out, 16)
                pool.wait_ge(s.tails_sb, 1)
                pool.dma_start(O["gdn_conv_prompt"][0, 0], tails_rows[0:3, :]).then_inc(s.out_c, 16)
                pool.dma_start(O["gdn_conv_sample"].rearrange("o b j c -> (o b j) c"), tails_rows[3:27, :]).then_inc(s.out_c, 16)
                pool.wait_ge(s.out_c, 32)
                pool.wait_ge(s.shift_out, 16 * (1 + NB))


            @block.tensor
            def _(pe):
                pe.sem_inc(s.pj, 2)

                def block_mm(u, it, n):
                    pe.wait_ge((s.w0, s.w1)[u], 16 * (it + 1))
                    pe.wait_ge(s.pj_evac, n + 1)
                    for c in range(3):
                        n = CH if c < 2 else CH + NB
                        for k in range(KD):
                            last = pe.matmul(ps[:, 3 * u + c, 0:n], wbuf[u][:, k, :], hT[:, k, c * CH:c * CH + n],
                                             start=(k == 0), stop=(k == KD - 1))
                    last.then_inc(s.pj, 1)

                with pe.Fori(0, NPQ // 2) as i:
                    for u in range(2):
                        block_mm(u, i, 2 * i + u)

                def norm_at(n, par, lhs, sq_count):
                    pe.wait_ge(s.sq, sq_count)
                    for c in range(3):
                        pe.wait_ge(s.nrm_ln, 3 * n + c + 1)
                        pe.matmul(ps[:, 6 + (3 * par + c) % 2, 0:CH], lhs, sq[:, c * CH:c * CH + CH],
                                  start=True, stop=True).then_inc(s.nrm, 1)

                with pe.Fori(0, NPC // 2) as i:
                    for u in range(2):
                        norm_at(2 * i + u, u, m.ones[:], 2 * i + u + 1)
                        block_mm(u, i + NPQ // 2, 2 * i + u + NPQ)
                pe.wait_ge(s.pj_evac, GATE_BLK + 1)
                for c in range(3):
                    for k in range(KD):
                        last = pe.matmul(ps[0:2 * H, c, 0:CH], wg[:, k, :], hT[:, k, c * CH:c * CH + CH],
                                         start=(k == 0), stop=(k == KD - 1))
                last.then_inc(s.pj, 1)
                pe.wait_ge(s.drv, 1)
                for j, (wt, lo, hi, blk, c0) in enumerate((
                        (lora, 0, 64, 6, 0), (lora, 0, 64, 6, 1), (lora, 64, 128, 6, 0), (lora, 64, 128, 6, 1),
                        (gup, 0, 128, 7, 0), (gup, 0, 128, 7, 1))):
                    u = (j + 1) % 2
                    pe.wait_ge(s.pj_evac, LORA_BLK + j + 1)
                    for c in range(3):
                        last = pe.matmul(ps[:, 3 * u + c, 0:CH], wt[lo:hi, c0 * P:c0 * P + P],
                                         cb[lo:hi, blk, c * CH:c * CH + CH], start=True, stop=True)
                    last.then_inc(s.pj, 1)
                for n in range(2):
                    norm_at(8 + n, n, m.blk64[:], 8 + n + 2)
                pe.wait_ge(s.gt_sb, 1)
                pe.wait_ge(s.nrm_ln, 3 * 10 + 2)
                for t in range(TILES):
                    n = P if t < NT else NS
                    last = pe.transpose(ps[0:n, 7, 8 * t:8 * t + 8], gt8[:, tokens(t):tokens(t) + n], m.ident[0:8, 0:8])
                last.then_inc(s.gt_T, 1)
                pe.wait_ge(s.pj_evac, TAIL_BLK + 2)
                pe.wait_ge(s.tails, 1)
                for b in range(12):
                    last = pe.transpose(ps[0:27, 3 + b // 4, (b % 4) * P:(b % 4) * P + P], tails[:, b, :], m.ident[:])
                last.then_inc(s.pj, 1)
                pe.wait_ge(s.tails_sb, 1)
                with pe.Fori(0, NPZ // 2) as i:
                    for u in range(2):
                        block_mm(u, i + (NPQ + NPC) // 2, 2 * i + u + Z_BLK - 1)
                pe.wait_ge(s.gt_ready, 1)
                g_p = g_all[:, 0:NT, :].rearrange("p t h -> p (t h)")
                pe.matmul(ps[:, 6, 0:32], m.causal[:], g_p, start=True, stop=True)
                pe.matmul(ps[0:NS, 6, 32:36], m.causal4[:], g_all[0:NS, NT, :], start=True, stop=True)
                pe.matmul(ps[:, 6, 64:96], m.ones[:], g_p, start=True, stop=True)
                pe.matmul(ps[0:NS, 6, 96:100], m.blk4[:], g_all[0:NS, NT, :], start=True, stop=True)
                pe.matmul(ps[:, 6, 128:160], m.ones[0:NS, :], gsel[:].rearrange("p b h -> p (b h)"), start=True, stop=True).then_inc(s.gb, 1)

            @block.scalar
            def _(act):
                act.sem_inc(s.pj_evac, 2)
                act.sem_inc(s.nrm_ln, 2)

                def evac_conv(u, i):
                    n = 2 * i + u
                    act.wait_ge(s.pj, n + 3)
                    act.wait_ge(s.conv, n + 1)
                    act.activation(pre[u][:, 3:3 + 2 * CH].rearrange("p (a n) -> p a n", n=CH), pbank(u)[:, 0:2, 0:CH], ACT.Copy)
                    act.activation(pre[u][:, 3 + 2 * CH:XB], pbank(u)[:, 2, 0:SEQ - 2 * CH], ACT.Copy)
                    act.activation(smp(pre[u], XB, 3 + TB, 0, 3), cst[:, ds(n, 1), :].rearrange("p o (b j) -> p (o b) j", j=3), ACT.Copy)
                    act.activation(smp(pre[u], XB, 3 + TB, 3, 3 + TB),
                                   pbank(u)[:, 2, SEQ - 2 * CH:CH].rearrange("p (b t) -> p b t", t=TB), ACT.Copy).then_inc(s.pj_evac, 1)

                act.wait_ge(s.zeroed, 1)
                with act.Fori(0, NPQ // 2) as i:
                    for u in range(2):
                        evac_conv(u, i)
                    for u in range(2):
                        act.wait_ge(s.conv, 2 * i + u + 3)
                        act.activation(qkv[:, ds(2 * i + u, 1), :], acc[u], ACT.Silu).then_inc(s.silu, 1)

                def square(n, src):
                    act.activation(sq, src, ACT.Square).then_inc(s.sq, 1)

                def norm_act(n, par, eps_scale):
                    act.wait_ge(s.nrm_done, n + 1)
                    for c in range(3):
                        act.wait_ge(s.nrm, 3 * n + c + 1)
                        act.activation(rs[:, c * CH:c * CH + CH], ps[:, 6 + (3 * par + c) % 2, 0:CH], ACT.Ln,
                                       bias=L2_EPS).then_inc(s.nrm_ln, 1)
                    act.drain()
                    act.activation(rs, rs, ACT.Exp, scale=-0.5).then_inc(s.rs, 1)

                act.preload_act_table_set(LNEXP)
                act.drain()
                square(0, qkv[:, 0, :])
                with act.Fori(0, NPC // 2) as i:
                    for u in range(2):
                        n = 2 * i + u
                        norm_act(n, u, None)
                        square(n + 1, qkv[:, ds(n + 1, 1), :])
                        act.wait_ge(s.pj, n + NPQ + 3)
                        act.wait_ge(s.mixd, n + 1)
                        act.activation(pre[u][:, 1:1 + 2 * CH].rearrange("p (a n) -> p a n", n=CH), pbank(u)[:, 0:2, 0:CH], ACT.Copy)
                        act.activation(pre[u][:, 1 + 2 * CH:1 + SEQ], pbank(u)[:, 2, 0:SEQ - 2 * CH], ACT.Copy)
                        act.activation(smp(pre[u], XB, 1 + TB, 0, 1), pbank(u)[:, 2, CH:CH + NB].rearrange("p (b j) -> p b j", j=1), ACT.Copy)
                        act.activation(smp(pre[u], XB, 1 + TB, 1, 1 + TB),
                                       pbank(u)[:, 2, SEQ - 2 * CH:CH].rearrange("p (b t) -> p b t", t=TB), ACT.Copy).then_inc(s.pj_evac, 1)
                act.wait_ge(s.mixd, NPC + 2)
                act.activation(cb[0:64, 6, :], cb[0:64, 6, :], ACT.Tanh)
                act.activation(cb[:, 7, :], cb[:, 7, :], ACT.Sigmoid).then_inc(s.drv, 1)
                act.wait_ge(s.pj, GATE_BLK + 3)
                act.activation(gt8.rearrange("p (a n) -> p a n", n=CH), ps[0:8, 0:3, 0:CH], ACT.Copy).then_inc(s.gt_sb, 1)
                act.drain()
                act.sem_inc(s.pj_evac, 1)
                for j in range(6):
                    u = (j + 1) % 2
                    act.wait_ge(s.pj, LORA_BLK + j + 3)
                    if j < 2:
                        act.wait_ge(s.mixd, NPC + 2)
                        dst, f, b = lw[:, j, :], ACT.Sigmoid, vec("rwkv_w0", j)
                    elif j < 4:
                        dst, f, b = bb[:, j - 2, :], ACT.Sigmoid, vec("rwkv_a0", j - 2)
                    else:
                        dst, f, b = cb[:, j + 2, :], ACT.Copy, 0.0
                        act.wait_ge(s.pj, LORA_BLK + 6 + 2)
                    act.activation(dst.rearrange("p (a n) -> p a n", n=CH), pbank(u)[:, :, 0:CH], f, bias=b).then_inc(s.pj_evac, 1)
                act.preload_act_table_set(LNEXP)
                for n in range(8, 10):
                    act.wait_ge(s.g_e, 2)
                    act.wait_ge(s.nrm, 3 * n)
                    act.activation(sq, kk[n - 8], ACT.Square).then_inc(s.sq, 1)
                    norm_act(n, n % 2, None)
                act.wait_ge(s.g_e, 3)
                act.activation(gtmp[:, 0], gtk[:, :, 0:H], ACT.Exp, scale=-1.0)
                act.activation(gts[:, 0, :], gts[:, 0, :], ACT.Exp)
                act.activation(gtmp[:, 2], gtmp[:, 1], ACT.Abs)
                act.drain()
                act.activation(gtmp[:, 2], gtmp[:, 2], ACT.Exp, scale=-1.0)
                act.drain()
                act.activation(gtmp[:, 2], gtmp[:, 2], ACT.Ln, bias=1.0).then_inc(s.gb, 1)
                act.wait_ge(s.out_c, 32)
                for j in range(4):
                    act.wait_ge(s.pj, Z_BLK + j + 3)
                    act.activation(zg[:, j, :].rearrange("p (a n) -> p a n", n=CH), pbank(j % 2)[:, :, 0:CH], ACT.Silu).then_inc(s.pj_evac, 1)
                act.wait_ge(s.gt_T, 1)
                for j in range(4):
                    act.wait_ge(s.pj, Z_BLK + 4 + j + 3)
                    dst = (ub if j < 2 else vbn)[:, j % 2, :]
                    act.activation(dst.rearrange("p (a n) -> p a n", n=CH), pbank(j % 2)[:, :, 0:CH], ACT.Gelu).then_inc(s.pj_evac, 1)
                act.preload_act_table_set(LNEXP)
                act.wait_ge(s.g_e, 4)
                act.activation(kdf[:], kdf[:], ACT.Exp)
                act.activation(gl_all[:, 0:NT, :].rearrange("p t h -> p (t h)"), ps[:, 6, 64:96], ACT.Exp)
                act.activation(glS[:].rearrange("p b h -> p (b h)"), ps[:, 6, 128:160], ACT.Exp)

            @block.vector
            def _(dve):
                dve.sem_inc(s.conv, 2)
                dve.sem_inc(s.mixd, 2)
                dve.sem_inc(s.nrm_done, 1)
                for u in range(2):
                    dve.memset(pre[u][:, 0:3], 0.0)
                dve.drain()
                dve.sem_inc(s.zeroed, 1)

                def conv(u, i):
                    n = 2 * i + u
                    dve.wait_ge(s.pj_evac, n + 3)
                    dve.tensor_copy(tails[:, ds(n, 1), 0:3], pre[u][:, SEQ:SEQ + 3])
                    dve.tensor_copy(tails[:, ds(n, 1), 3:27].rearrange("p o (b j) -> p (o b) j", j=3), smp(pre[u], XB, 3 + TB, TB, TB + 3))
                    dve.wait_ge(s.silu, n + 1)
                    a_p, a_s = acc[u][:, 0:SEQ], acc[u][:, SEQ:NTOK].rearrange("p (b t) -> p b t", t=TB)
                    for j in range(CW):
                        wv = vecs[:, ds(ROWS["gdn_conv_w"][0] + 12 * j + n, 1)]
                        x_p, x_s = pre[u][:, j:j + SEQ], smp(pre[u], XB, 3 + TB, j, j + TB)
                        if j == 0:
                            dve.tensor_scalar(a_p, x_p, wv, None, ALU.mult)
                            last = dve.tensor_scalar(a_s, x_s, wv, None, ALU.mult)
                        else:
                            dve.drain()
                            dve.scalar_tensor_tensor(a_p, x_p, wv, a_p, ALU.mult, ALU.add)
                            last = dve.scalar_tensor_tensor(a_s, x_s, wv, a_s, ALU.mult, ALU.add)
                    last.then_inc(s.conv, 1)

                dve.sem_inc(s.silu, 2)
                with dve.Fori(0, NPQ // 2) as i:
                    for u in range(2):
                        conv(u, i)
                dve.drain()
                dve.sem_inc(s.tails, 1)

                def normalise(n, scale, dst, src):
                    dve.wait_ge(s.rs, n + 1)
                    dve.scalar_tensor_tensor(dst, src, scale, rs, ALU.mult, ALU.mult).then_inc(s.nrm_done, 1)

                for half, scale in ((0, HA ** -0.5), (1, 1.0)):
                    with dve.Fori(2 * half, 2 * half + 2) as i:
                        for u in range(2):
                            n = 2 * i + u
                            normalise(n, scale, qkv[:, ds(n, 1), :], qkv[:, ds(n, 1), :])
                            dve.drain()
                            dve.wait_ge(s.pj_evac, n + NPQ + 3)
                            mu = vecs[:, ds(ROWS["rwkv_mu"][0] + n, 1)]
                            cur, prv = pre[u][:, 1:1 + SEQ], pre[u][:, 0:SEQ]
                            cur_s, prv_s = smp(pre[u], XB, 1 + TB, 1, 1 + TB), smp(pre[u], XB, 1 + TB, 0, TB)
                            d_s = dtmp[:, SEQ:NTOK].rearrange("p (b t) -> p b t", t=TB)
                            dve.tensor_tensor(dtmp[:, 0:SEQ], prv, cur, ALU.subtract)
                            dve.tensor_tensor(d_s, prv_s, cur_s, ALU.subtract)
                            dve.drain()
                            dve.scalar_tensor_tensor(cb[:, ds(n, 1), 0:SEQ], dtmp[:, 0:SEQ], mu, cur, ALU.mult, ALU.add)
                            dve.scalar_tensor_tensor(cb[:, ds(n, 1), SEQ:NTOK].rearrange("p o (b t) -> p (o b) t", t=TB), d_s, mu, cur_s,
                                                     ALU.mult, ALU.add).then_inc(s.mixd, 1)
                dve.drain()
                for c in range(2):
                    dve.tensor_scalar(kk[c], cb[:, 2 + c, :], vec("rwkv_k_k", c), None, ALU.mult)
                dve.wait_ge(s.pj_evac, LORA_BLK + 4 + 2)
                for c in range(2):
                    dve.tensor_scalar(acc[c],
 bb[:, c, :], vec("rwkv_k_a", c), m.omka[:, c:c + 1], ALU.mult, ALU.add)
                dve.drain()
                for c in range(2):
                    dve.tensor_tensor(cb[:, 2 + c, :], cb[:, 2 + c, :], acc[c], ALU.mult).then_inc(s.g_e, 1)
                for n in range(2):
                    normalise(8 + n, 1.0, kk[n], kk[n])
                dve.drain()
                for n in range(2):
                    dve.tensor_tensor(bb[:, n, :], bb[:, n, :], kk[n], ALU.mult)
                dve.wait_ge(s.gt_T, 1)
                dve.tensor_copy(gtk[:].rearrange("p t c -> p (t c)")[:, 0:64], ps[:, 7, 0:64])
                dve.memset(gtk[:, NT, :], 0.0)
                dve.drain()
                dve.tensor_copy(gtk[0:NS, NT, :], ps[0:NS, 7, 64:72])
                dve.drain()
                dve.tensor_tensor(gtmp[:, 1], gtk[:, :, H:2 * H], bc(gts[:, 1, :], 1, TILES), ALU.add).then_inc(s.g_e, 1)
                dve.wait_ge(s.pj, TAIL_BLK + 3)
                dve.tensor_copy(tails_rows, ps[0:27, 3:6, :].rearrange("p a n -> p (a n)")).then_inc(s.tails_sb, 1)
                dve.wait_ge(s.gb, 1)
                dve.tensor_scalar(gtmp[:, 0], gtmp[:, 0], 1.0, None, ALU.add)
                dve.tensor_scalar(gtmp[:, 1], gtmp[:, 1], 0.0, None, ALU.max)
                dve.drain()
                dve.reciprocal(beta_all[:], gtmp[:, 0])
                dve.tensor_tensor(gtmp[:, 1], gtmp[:, 1], gtmp[:, 2], ALU.add)
                dve.drain()
                dve.scalar_tensor_tensor(g_all[:], gtmp[:, 1], -1.0, bc(gts[:, 0, :], 1, TILES), ALU.mult, ALU.mult)
                dve.drain()
                dve.tensor_tensor(gsel[:], bc(g_all[0:NS, NT, :], 1, NB), bc(m.seq4[:], 2, H), ALU.mult).then_inc(s.gt_ready, 1)
                dve.wait_ge(s.gb, 2)
                dve.tensor_copy(gcum[:, 0:NT, :].rearrange("p t h -> p (t h)"), ps[:, 6, 0:32])
                dve.tensor_copy(gcum[0:NS, NT, :], ps[0:NS, 6, 32:36])
                dve.memset(kdf[:, NT, :], 0.0)
                dve.drain()
                dve.tensor_tensor(kdf[:, 0:NT, :].rearrange("p t h -> p (t h)"), ps[:, 6, 64:96], gcum[:, 0:NT, :].rearrange("p t h -> p (t h)"), ALU.subtract)
                dve.tensor_tensor(kdf[0:NS, NT, :], ps[0:NS, 6, 96:100], gcum[0:NS, NT, :], ALU.subtract).then_inc(s.g_e, 1)
        pst.close()
        p1.close()
        spatial_gating(nc, O, sems("g_", SGU_SEMS), ps, m, ub, vbn, sguT, sgb, lnwb)
        v_stack.close()
        g = Names(qkv=qkv, zg=zg, ub=ub, cb=cb, lw=lw, bb=bb, kk=kk, vec=vec, g_all=g_all, beta_all=beta_all,
                            gcum=gcum, kdf=kdf, gl_all=gl_all, glS=glS)
        tile_sems = sems("t_", TSEMS)
        tile_stage(nc, A, O, Names(**tile_sems, **sems("tp_", STAGE_SEMS)), ps, m, g, False)
        tile_stage(nc, A, O, Names(**tile_sems, **sems("ts_", STAGE_SEMS)), ps, m, g, True)
        F = Ctx(nc, root)
        xy = F.sb("residual", P, TILES, D)
        route = Names(w=F.sb("choice_weights", P, 2, TILES), slot=F.sb("choice_slots", P, 2, TILES, dt=U32),
                      token=F.sb("slot_tokens", P, SLOTS + 1, dt=U32), first=F.sb("first_slot_tile", P, NE + 1, dt=U32))
        h2_rows = nc.dram_tensor("h2_rows", [NTOK, D], F32, kind="Internal").ap()
        y_rows = nc.dram_tensor("expert_rows", [(SLOTS + 1) * P, D], F32, kind="Internal").ap()
        h2T = [ub[:, 0, :], ub[:, 1, :], lw[:, 0, :], lw[:, 1, :], bb[:, 0, :], bb[:, 1, :], kk[0], kk[1]]
        out_projection(nc, A, sems("o_", OUT_SEMS), ps, m, g, h2T, xy, route, h2_rows)
        experts(nc, A, sems("e_", MOE_SEMS), ps, m, g, route, h2_rows, y_rows)
        combine(nc, A, O, sems("f_", FIN_SEMS), g, xy, route, y_rows)
        if debug:
            debug(nc, locals())


def spatial_gating(nc, O, sem, ps, m, ub, vbn, sguT, sgb, lnwb):
    with ExitStack() as st:
        T = Ctx(nc, st)
        vc = [T.sb(f"v_centred_{u}", P, 4, H, HC) for u in range(2)]
        sqv = [T.sb(f"v_squares_{u}", P, 4, H, HC) for u in range(2)]
        st4 = [T.sb(f"v_stats_{u}", P, 2, 4, H) for u in range(2)]
        batches = [(0, 4, P), (4, 4, P), (NT, 1, NS)]

        def flat(a, n, k):
            return a[0:n].rearrange("p t h d -> p (t h d)")[:, 0:k * DB]

        with nc.Block() as block:
            @block.tensor
            def _(pe):
                def transposes(i):
                    t0, k, n = batches[i]
                    b = 4 * (i % 2)
                    if i == 2:
                        pe.wait_ge(sem.vn, 1)
                    for j in range(k):
                        for c in range(2):
                            last = pe.transpose(ps[0:n, b + j // 2, (j % 2) * DB + c * P:(j % 2) * DB + c * P + P],
                                                vbn[:, c, tokens(t0 + j):tokens(t0 + j) + n], m.ident[:])
                    last.then_inc(sem.vT, 1)

                def mix(i):
                    t0, k, n = batches[i]
                    b = 4 * (i % 2) + 2
                    pe.wait_ge(sem.vn, i + 1)
                    if i == 2:
                        pe.wait_ge(sem.vout, 1)
                    w = sguT if n == P else m.sguS
                    for j in range(k):
                        for h in range(H):
                            last = pe.matmul(ps[64 * (h % 2):64 * (h % 2) + 64, b + j // 2, (j % 2) * 256 + (h // 2) * P:(j % 2) * 256 + (h // 2) * P + n],
                                             vc[i % 2][0:n, j, h, :], w[0:n, h, :], start=True, stop=True)
                    last.then_inc(sem.mix, 1)

                transposes(0)
                transposes(1)
                mix(0)
                transposes(2)
                mix(1)
                mix(2)

            @block.scalar
            def _(act):
                for i, (t0, k, n) in enumerate(batches):
                    v = st4[i % 2][0:n, 1].rearrange("p t h -> p (t h)")[:, 0:k * H]
                    act.wait_ge(sem.var, i + 1)
                    act.activation(v, v, ACT.Ln, scale=1.0 / HC, bias=LN_EPS)
                    act.drain()
                    act.activation(v, v, ACT.Exp, scale=-0.5).then_inc(sem.rstd, 1)

            @block.vector
            def _(dve):
                def centre(i):
                    t0, k, n = batches[i]
                    u = i % 2
                    src = ps[0:n, 4 * u:4 * u + 2, :].rearrange("p a (h d) -> p (a h) d", d=HC)[:, 0:k * H, :]
                    mu = st4[u][0:n, 0].rearrange("p t h -> p (t h)")[:, 0:k * H]
                    var = st4[u][0:n, 1].rearrange("p t h -> p (t h)")[:, 0:k * H]
                    c3 = flat(vc[u], n, k).rearrange("p (h d) -> p h d", d=HC)
                    s3 = flat(sqv[u], n, k).rearrange("p (h d) -> p h d", d=HC)
                    dve.wait_ge(sem.vT, i + 1)
                    dve.tensor_reduce(mu, src, AX_X, ALU.add)
                    dve.drain()
                    dve.tensor_scalar(mu, mu, 1.0 / HC, None, ALU.mult)
                    dve.drain()
                    if i == 2:
                        dve.wait_ge(sem.mix, 1)
                    dve.tensor_tensor(c3, src, bc(mu, 2, HC), ALU.subtract)
                    dve.drain()
                    dve.tensor_tensor(s3, c3, c3, ALU.mult)
                    dve.drain()
                    dve.tensor_reduce(var, s3, AX_X, ALU.add).then_inc(sem.var, 1)

                def scale(i):
                    t0, k, n = batches[i]
                    u = i % 2
                    var = st4[u][0:n, 1].rearrange("p t h -> p (t h)")[:, 0:k * H]
                    c3 = flat(vc[u], n, k).rearrange("p (h d) -> p h d", d=HC)
                    c2 = flat(vc[u], n, k).rearrange("p (t c) -> p t c", c=DB)
                    dve.drain()
                    dve.wait_ge(sem.rstd, i + 1)
                    dve.tensor_tensor(c3, c3, bc(var, 2, HC), ALU.mult)
                    dve.drain()
                    dve.tensor_tensor(c2, c2, bc(lnwb[0:n, 0, :], 1, k), ALU.mult)
                    dve.drain()
                    dve.tensor_tensor(c2, c2, bc(lnwb[0:n, 1, :], 1, k), ALU.add).then_inc(sem.vn, 1)

                def gate(i):
                    t0, k, n = batches[i]
                    u = i % 2
                    dve.wait_ge(sem.mix, i + 1)
                    for c in range(2):
                        o = sqv[u][:].rearrange("p t h d -> p (t h d)")[:, c * 512:c * 512 + k * n]
                        src = ps[:, 4 * u + 2:4 * u + 4, :].rearrange("p a (j c n) -> p (a j) c n", j=2, c=2)[:, 0:k, c, 0:n]
                        dst = ub[:, c, tokens(t0):tokens(t0) + k * n]
                        if n == P:
                            dve.tensor_tensor(o.rearrange("p (j n) -> p j n", n=n), src, bc(sgb[:, c, :], 1, k), ALU.add)
                        else:
                            dve.tensor_tensor(o.rearrange("p (b t) -> p b t", t=TB), src.rearrange("p j (b t) -> p (j b) t", t=TB),
                                              bc(sgb[:, c, 0:TB], 1, NB), ALU.add)
                        dve.drain()
                        last = dve.tensor_tensor(dst, dst, o, ALU.mult)
                    last.then_inc(sem.vout, 1)

                centre(0)
                centre(1)
                scale(0)
                scale(1)
                gate(0)
                dve.drain()
                centre(2)
                gate(1)
                scale(2)
                gate(2)

            @block.sync
            def _(sp):
                sp.wait_ge(sem.vn, 3)
                sp.dma_start(O["chunk_v_sample"][0].rearrange("b t c -> (b t) c"),
                             vc[0][0:NS, 0].rearrange("p h d -> p (h d)")).then_inc(sem.rows_out, 16)
                sp.wait_ge(sem.rows_out, 16)


TSEMS = """gub rows kvT erow kbt dtp dexp gram ltA kqd c0A c0TA t1A YA VA TTA TA TtA ckA
ks X vn vnew o dS Sup sqo osum ors odone
scan aex e123 rkb krk tokT tokc gramK evK gramB ltC c0C c0TC t1C YC VC TTC TC TtC ckC
xq xc pp pc dz z y1 ymu yc sqy yvar yrs bon rkr tile_end""".split()
STAGE_SEMS = "ld st_T fin outp".split()


def tile_stage(nc, A, O, s, ps, m, g, sample):
    with ExitStack() as st:
        B = Ctx(nc, st)
        n = NS if sample else P
        x = "s_" if sample else "p_"
        sb = lambda name, *shape: B.sb(x + name, *shape)
        cs, ncs = (NS, 1) if sample else (64, 2)
        MA, MC = 7, 6
        LA, LC = (2, 2) if sample else (MA, MC)
        causal = m.causal4 if sample else m.causal
        rwm = m.rw4 if sample else m.rw
        reset = m.reset4 if sample else m.reset

        kst, vst = sb("k_tile", P, H, n), sb("v_tile", P, H, n)
        gub = sb("gate_rows_in", n, 2, H, n)
        DT, LTA = gub[:, 0], gub[:, 1]
        erow, kbT, qdT = sb("e_gc_rows", P, H, n), sb("kbT", P, H, n), sb("qdT", P, H, n)
        kbdT = sb("kbdT", P, H, n) if sample else vst
        atT = sb("attnT", n, H, n)
        vb, kdec = sb("v_beta", n, H, HA), sb("k_dec", n, H, HA)
        rsA = sb("o_rstd", P, H, n) if sample else vb
        ckA = [sb(f"ckA_{u}", n, H, n) for u in range(2)]
        VA, TA, TTA = (sb(k, n, H, n) for k in ("VA", "TA", "TTA"))
        if sample:
            XA, vnew, sqo = sb("XA", n, H, HA), sb("vnew", n, H, HA), sb("sqo", P, H, n)
        else:
            XA, vnew, sqo = ckA[0], VA, TA
        t1 = kbT
        KR, KB = sb("KR", P, 2, 2, n), sb("KB", P, 2, 2, n)
        ac, ax, e2 = (sb(k, P, 2, n) for k in ("acum", "aexc", "e_minus"))
        el = sb("chunk_decay_c", P, 2, NB)
        vct = sb("vc_tile", P, 2, n)
        MR, LB = sb("MR", n, H, 2, n), sb("LB", n, H, 2, n)
        tokKB, tokV = sb("tokKB", n, 2, 2, P), sb("tokV", n, 2, P)
        ckC = [sb(f"ckC_{u}", n, H, n) for u in range(2)]
        VC, TC, TTC = (sb(k, n, H, n) for k in ("VC", "TC", "TTC"))
        if sample:
            XC, PC = sb("XC", n, 2, P), sb("PC", n, 2, P)
            rk = sb("rk", P, 2, n)
            half = lambda p, blk, b: g.qkv[0:p, blk + b // 2, (b % 2) * 512:(b % 2) * 512 + 512]
            S = [half(P, 8, b).rearrange("p (h v) -> p h v", h=H) for b in range(NB)]
            kdm = [half(n, 0, b).rearrange("p (h v) -> p h v", h=H) for b in range(NB)]
            kbm_tok = [half(n, 4, b) for b in range(NB)]
            Z = sb("Z", P, NB, 2, P)
            kbm = sb("kb_masked", P, H, 36 * NB)
            krm = sb("kk_masked", P, 2, 36 * NB)
            zin = sb("z_rows", P, NB, 2, P)
        else:
            XC = ckC[0][:].rearrange("p h n -> p (h n)")[:, 0:256].rearrange("p (c n) -> p c n", c=2)
            PC = VC[:].rearrange("p h n -> p (h n)")[:, 0:256].rearrange("p (c n) -> p c n", c=2)
            rk = ckC[1][:].rearrange("p h n -> p (h n)")[:, 0:256].rearrange("p (c n) -> p c n", c=2)
            S = sb("S", P, H, HA)
            Z = sb("Z", P, 2, 2, P)
            zin = sb("z_rows", P, 2, P)
        ztmp = sb("z_tmp", P, 2, HC)
        LTC = LB[:, :, 0, :]

        def bank(b, rows=n, cols=n):
            return ps[0:rows, b, :].rearrange("p (h x) -> p h x", h=H)[:, :, 0:cols]

        def rows_of(b, p):
            return ps[0:p, b, 0:H * n].rearrange("p (h n) -> p h n", h=H)

        def loop(eng, body):
            def one(t, cols):
                body(t, cols)
                eng.drain()
                eng.sem_inc(s.tile_end, 1)
                eng.wait_ge(s.tile_end, 4 * (t + 1))
            if sample:
                body(NT, slice(SEQ, NTOK))
            else:
                with eng.Fori(0, NT) as t:
                    one(t, ds(t * P, P))

        def gate(a, t):
            return a[0:n, NT, :] if sample else a[:, ds(t, 1), :].rearrange("p o h -> p (o h)")

        def gate1(a, t, h):
            return a[0:n, NT, h:h + 1] if sample else a[:, ds(t, 1), h:h + 1].rearrange("p o h -> p (o h)")

        with nc.Block() as block:
            @block.gpsimd
            def _(pool):
                if not sample:
                    pool.memset(S[:], 0.0)
                    pool.memset(Z[:], 0.0)
                else:
                    pool.memset(kbm[:], 0.0)
                    pool.memset(krm[:], 0.0)
                    pool.memset(zin[:], 0.0)
                    pool.drain()
                pool.sem_inc(s.ld, 1)

                def body(t, c):
                    pool.tensor_copy(vct[:], g.cb[:, 4:6, c])
                    pool.tensor_copy(kst[:], g.qkv[:, 4:8, c])
                    pool.tensor_copy(vst[:], g.qkv[:, 8:12, c])
                    pool.wait_ge(s.scan, t + 1)
                    pool.tensor_tensor(ax[:], ac[:], g.lw[:, :, c], ALU.subtract).then_inc(s.aex, 1)
                    pool.wait_ge(s.e123, t + 1)
                    pool.tensor_tensor(KB[:, :, 0, :], g.cb[:, 2:4, c], e2[:], ALU.mult)
                    pool.tensor_tensor(KB[:, :, 1, :], g.bb[:, :, c], e2[:], ALU.mult).then_inc(s.rkb, 1)
                    for j in range(2):
                        pool.tensor_tensor(KR[:, j, 0, :], g.kk[j][:, c], ax[:, j, :], ALU.mult)
                    pool.tensor_tensor(KR[:, :, 1, :], g.cb[:, 0:2, c], ac[:], ALU.mult)
                    last = pool.tensor_copy(el[:, :, 0:n // (TB if sample else 64)],
                                            ac[:].rearrange("p c (k x) -> p c k x", x=TB if sample else 64)[:, :, :, (TB if sample else 64) - 1])
                    if sample:
                        pool.drain()
                        last = pool.tensor_copy(krm[:].rearrange("p c (b x) -> p c b x", x=36)[:, :, :, 0:TB],
                                                KR[:, :, 0, :].rearrange("p c (b t) -> p c b t", t=TB))
                    last.then_inc(s.krk, 1)
                    pool.wait_ge(s.ltC, t + 1)
                    pool.tensor_tensor(ckC[0][:], LTC, bc(m.lev[0:n, 0, 0:n], 1, H), ALU.mult).then_inc(s.c0C, 1)
                    pool.drain()
                    pool.tensor_tensor(TTC[:], bc(m.ident[0:n, 0:n], 1, H), ckC[0][:], ALU.subtract)
                    pool.tensor_tensor(ckC[1][:], LTC, bc(m.lev[0:n, 1, 0:n], 1, H), ALU.mult).then_inc(s.ckC, 1)
                    pool.wait_ge(s.ltA, t + 1)
                    pool.tensor_tensor(ckA[0][:], LTA, bc(m.lev[0:n, 0, 0:n], 1, H), ALU.mult).then_inc(s.c0A, 1)
                    pool.drain()
                    pool.tensor_tensor(TTA[:], bc(m.ident[0:n, 0:n], 1, H), ckA[0][:], ALU.subtract)
                    pool.tensor_tensor(ckA[1][:], LTA, bc(m.lev[0:n, 1, 0:n], 1, H), ALU.mult).then_inc(s.ckA, 1)
                    pool.wait_ge(s.kbt, t + 1)
                    pool.wait_ge(s.erow, t + 1)
                    pool.wait_ge(s.kvT, t + 1)
                    pool.tensor_tensor(kbdT[:], kbT[:], erow[:], ALU.mult)
                    last = pool.tensor_tensor(qdT[:], g.qkv[:, 0:4, c], erow[:], ALU.mult)
                    if sample:
                        pool.drain()
                        last = pool.tensor_copy(kbm[:].rearrange("p c (b x) -> p c b x", x=36)[:, :, :, 0:TB],
                                                kbdT[:].rearrange("p c (b t) -> p c b t", t=TB))
                    last.then_inc(s.kqd, 1)
                    for k in range(2, 7):
                        if k < LC:
                            if k == 2:
                                pool.drain()
                                pool.wait_ge(s.t1C, t + 1)
                            else:
                                pool.wait_ge(s.YC, (MC - 1) * t + k - 2)
                            pool.tensor_tensor(ckC[k % 2][:], LTC, bc(m.lev[0:n, k, 0:n], 1, H), ALU.mult).then_inc(s.ckC, 1)
                        if k < LA:
                            if k == 2:
                                pool.drain()
                                pool.wait_ge(s.t1A, t + 1)
                            else:
                                pool.wait_ge(s.YA, (MA - 1) * t + k - 2)
                            pool.tensor_tensor(ckA[k % 2][:], LTA, bc(m.lev[0:n, k, 0:n], 1, H), ALU.mult).then_inc(s.ckA, 1)
                    if sample:
                        pool.wait_ge(s.kbt, t + 1)
                        for b in range(NB):
                            pool.tensor_scalar(kdm[b], kdec[:], m.seq4[:, b:b + 1], None, ALU.mult)
                        pool.wait_ge(s.tokc, t + 1)
                        for b in range(NB):
                            last = pool.tensor_scalar(kbm_tok[b], tokKB[:].rearrange("p a b n -> p (a b n)"),
                                                      m.seq4[:, b:b + 1], None, ALU.mult)
                        last.then_inc(s.rkr, 1)

                loop(pool, body)

            @block.tensor
            def _(pe):
                if sample:
                    pe.wait_ge(s.outp, 16 * (NB + 4))
                    for b in range(NB):
                        for c in range(2):
                            q = 2 * b + c
                            last = pe.transpose(ps[:, 4 + q // 4, (q % 4) * P:(q % 4) * P + P], zin[:, b, c, :], m.ident[:])
                    last.then_inc(s.st_T, 1)
                    pe.wait_ge(s.fin, 1)
                pe.wait_ge(s.ld, 1)

                def body(t, c):
                    now = t + 1
                    pe.wait_ge(s.rkb, now)
                    for j in range(2):
                        for y in range(2):
                            pe.transpose(ps[0:n, 0, (2 * j + y) * P:(2 * j + y) * P + P], KB[:, j, y, :], m.ident[:])
                    for j in range(2):
                        last = pe.transpose(ps[0:n, 1, j * P:j * P + P], vct[:, j, :], m.ident[:])
                    last.then_inc(s.tokT, 1)
                    pe.wait_ge(s.krk, now)

                    def gram(y, b0):
                        for h in range(H):
                            r = slice(64 * (h % 2), 64 * (h % 2) + 64)
                            last = pe.matmul(ps[0:n, b0 + h % 2, (h // 2) * 2 * n:(h // 2) * 2 * n + 2 * n], KB[r, h // 2, y, :],
                                             KR[r, h // 2, :, :].rearrange("p a n -> p (a n)"), start=True, stop=True)
                        return last

                    gram(0, 2).then_inc(s.gramK, 1)
                    pe.wait_ge(s.gub, now)
                    pe.matmul(ps[:, 4, 0:H * n], m.ones[0:n, :], gub[:, 1].rearrange("p h n -> p (h n)"), start=True, stop=True)
                    pe.matmul(ps[:, 5, 0:H * n], m.ones[0:n, :], gub[:, 0].rearrange("p h n -> p (h n)"), start=True, stop=True)\
                        .then_inc(s.rows, 1)
                    for h in range(H):
                        pe.transpose(ps[0:n, 6, h * P:h * P + P], kst[:, h, :], m.ident[:])
                    for h in range(H):
                        last = pe.transpose(ps[0:n, 7, h * P:h * P + P], vst[:, h, :], m.ident[:])
                    last.then_inc(s.kvT, 1)
                    pe.wait_ge(s.tokc, now)
                    gram(1, 0).then_inc(s.gramB, 1)
                    pe.wait_ge(s.kbt, now)
                    pe.wait_ge(s.dtp, now)
                    for h in range(H):
                        pe.matmul(bank(4)[:, h, :], kst[:, h, :], kbT[:, h, :], start=True, stop=True)
                        last = pe.matmul(bank(5)[:, h, :], kst[:, h, :], g.qkv[:, h, c], start=True, stop=True)
                    last.then_inc(s.gram, 1)

                    def first(ck, b, ready, done):
                        pe.wait_ge(ready, now)
                        for h in range(H):
                            last = pe.transpose(bank(b)[:, h, :], ck[:, h, :], m.ident[0:n, 0:n])
                        last.then_inc(done, 1)

                    def y_mm(ck, T, b, done):
                        for h in range(H):
                            last = pe.matmul(bank(b)[:, h, :], ck[:, h, :], T[:, h, :], start=True, stop=True)
                        last.then_inc(done, 1)

                    def t_mm(V, TT, b, lastlevel, done):
                        if not lastlevel:
                            for h in range(H):
                                pe.matmul(bank(b)[:, h, :], TT[:, h, :], V[:, h, :], start=True, stop=True)
                        for h in range(H):
                            last = pe.matmul(bank(b + 1)[:, h, :], V[:, h, :], TT[:, h, :], start=True, stop=True)
                        last.then_inc(done, 1)

                    pe.wait_ge(s.evK, now)
                    first(ckC[0], 2, s.c0C, s.c0TC)
                    pe.wait_ge(s.ltC, now)
                    first(ckA[0], 0, s.c0A, s.c0TA)
                    for k in range(1, max(LA, LC)):
                        if k < LC:
                            w = (MC - 1) * t + k
                            pe.wait_ge(s.ckC, w)
                            if k == 1:
                                pe.wait_ge(s.t1C, now)
                            else:
                                pe.wait_ge(s.TC, (MC - 2) * t + k - 1)
                                pe.wait_ge(s.TtC, w - 1)
                            y_mm(ckC[k % 2], TC, 2, s.YC)
                        if k < LA:
                            w = (MA - 1) * t + k
                            pe.wait_ge(s.ckA, w)
                            if k == 1:
                                pe.wait_ge(s.t1A, now)
                            else:
                                pe.wait_ge(s.TA, (MA - 2) * t + k - 1)
                                pe.wait_ge(s.TtA, w - 1)
                            y_mm(ckA[k % 2], TA, 0, s.YA)
                        if k < LC:
                            pe.wait_ge(s.VC, (MC - 1) * t + k)
                            t_mm(VC, TTC, 2, k == LC - 1, s.TTC)
                        if k < LA:
                            pe.wait_ge(s.VA, (MA - 1) * t + k)
                            t_mm(VA, TTA, 0, k == LA - 1, s.TTA)

                    def rwkv_x(cc):
                        r = slice(cs * cc, cs * cc + cs)
                        for j in range(2):
                            for x_ in range(2):
                                hp = slice(64 * x_, 64 * x_ + 64)
                                o = ps[r, 2, j * P + 64 * x_:j * P + 64 * x_ + 64]
                                if sample:
                                    for b in range(NB):
                                        pe.matmul(o, krm[:, j, NS * b:NS * b + NS], Z[:, b, j, hp], start=(b == 0), stop=False)
                                else:
                                    pe.matmul(o, KR[:, j, 0, r], Z[:, cc, j, hp], start=True, stop=False)
                                last = pe.matmul(o, MR[:, 2 * j + x_, 0, r], tokV[:, j, hp], start=False, stop=True)
                        last.then_inc(s.xq, 1)

                    def rwkv_p(cc):
                        r = slice(cs * cc, cs * cc + cs)
                        pe.wait_ge(s.xc, 2 * t + cc + 1)
                        for h in range(H):
                            last = pe.matmul(ps[r, 3, h * HC:h * HC + HC], TTC[:, h, r], XC[:, h // 2, 64 * (h % 2):64 * (h % 2) + 64],
                                             start=True, stop=True)
                        last.then_inc(s.pp, 1)

                    def rwkv_dz(cc):
                        r = slice(cs * cc, cs * cc + cs)
                        pe.wait_ge(s.pc, 2 * t + cc + 1)
                        if not sample:
                            for j in range(2):
                                o = ps[:, 2, 256 + j * P:256 + j * P + P]
                                pe.matmul(o, tokKB[r, j, 0, :], tokV[r, j, :], start=True, stop=False)
                                last = pe.matmul(o, tokKB[r, j, 1, :], PC[r, j, :], start=False, stop=True)
                            last.then_inc(s.dz, 1)
                        else:
                            pe.wait_ge(s.rkr, 1)
                            for b in range(NB):
                                if b >= 2:
                                    pe.wait_ge(s.z, 2 * t + b - 1)
                                for j in range(2):
                                    o = ps[:, (2, 6)[b % 2], 256 + j * P:256 + j * P + P]
                                    pe.matmul(o, kbm_tok[b][:, 2 * j * P:2 * j * P + P], tokV[:, j, :], start=True, stop=False)
                                    last = pe.matmul(o, kbm_tok[b][:, 2 * j * P + P:2 * j * P + 2 * P], PC[:, j, :], start=False, stop=True)
                                last.then_inc(s.dz, 1)

                    def rwkv_y(cc):
                        r = slice(cs * cc, cs * cc + cs)
                        pe.wait_ge(s.pc, 2 * t + cc + 1)
                        for h in range(H):
                            hp = slice(64 * (h % 2), 64 * (h % 2) + 64)
                            o = ps[hp, 3, 256 + (h // 2) * n + cs * cc:256 + (h // 2) * n + cs * cc + cs]
                            if sample:
                                for b in range(NB):
                                    q = slice(TB * b, TB * b + TB)
                                    pe.matmul(o[:, q], tokV[:, h // 2, hp], MR[:, h, 1, q], start=True, stop=False)
                                    pe.matmul(o[:, q], PC[:, h // 2, hp], LB[:, h, 1, q], start=False, stop=False)
                                    last = pe.matmul(o[:, q], Z[:, b, h // 2, hp], KR[:, h // 2, 1, q], start=False, stop=True)
                            else:
                                pe.matmul(o, tokV[:, h // 2, hp], MR[:, h, 1, r], start=True, stop=False)
                                pe.matmul(o, PC[:, h // 2, hp], LB[:, h, 1, r], start=False, stop=False)
                                last = pe.matmul(o, Z[:, cc, h // 2, hp], KR[:, h // 2, 1, r], start=False, stop=True)
                        last.then_inc(s.y1, 1)

                    pe.wait_ge(s.kqd, now)
                    if not sample:
                        pe.wait_ge(s.Sup, now)
                    for h in range(H):
                        o = bank(6, cols=P)[:, h, :]
                        if sample:
                            for b in range(NB):
                                last = pe.matmul(o, kbm[:, h, NS * b:NS * b + NS], S[b][:, h, :], start=(b == 0), stop=(b == NB - 1))
                        else:
                            last = pe.matmul(o, kbdT[:, h, :], S[:, h, :], start=True, stop=True)
                    last.then_inc(s.ks, 1)
                    if sample:
                        rwkv_x(0)
                    else:
                        pe.wait_ge(s.TtC, (MC - 1) * t + LC - 1)
                        rwkv_x(0)
                    pe.wait_ge(s.TtA, (MA - 1) * t + LA - 1)
                    pe.wait_ge(s.X, now)
                    for h in range(H):
                        last = pe.matmul(bank(7, cols=P)[:, h, :], TTA[:, h, :], XA[:, h, :], start=True, stop=True)
                    last.then_inc(s.vn, 1)
                    pe.wait_ge(s.TtC, (MC - 1) * t + LC - 1)
                    rwkv_p(0)
                    pe.wait_ge(s.vnew, now)
                    for h in range(H):
                        o = bank(4, rows=P)[:, h, :]
                        if sample:
                            for b in range(NB):
                                q = slice(TB * b, TB * b + TB)
                                pe.matmul(o[:, q], vnew[:, h, :], atT[:, h, q], start=True, stop=False)
                                last = pe.matmul(o[:, q], S[b][:, h, :], qdT[:, h, q], start=False, stop=True)
                        else:
                            pe.matmul(o, vnew[:, h, :], atT[:, h, :], start=True, stop=False)
                            last = pe.matmul(o, S[:, h, :], qdT[:, h, :], start=False, stop=True)
                    last.then_inc(s.o, 1)
                    if not sample:
                        for h in range(H):
                            last = pe.matmul(bank(5, rows=P)[:, h, :], kdec[:, h, :], vnew[:, h, :], start=True, stop=True)
                        last.then_inc(s.dS, 1)
                    else:
                        pe.wait_ge(s.rkr, 1)
                        for b in range(NB):
                            if b >= 2:
                                pe.wait_ge(s.Sup, t + b)
                            for h in range(H):
                                last = pe.matmul(ps[:, (5, 7)[b % 2], h * P:h * P + P], kdm[b][:, h, :], vnew[:, h, :], start=True, stop=True)
                            last.then_inc(s.dS, 1)
                    if sample:
                        rwkv_y(0)
                        rwkv_dz(0)
                    else:
                        rwkv_dz(0)
                        rwkv_y(0)
                        pe.wait_ge(s.z, 2 * t + 1)
                        rwkv_x(1)
                    if sample:
                        pe.wait_ge(s.z, 2 * t + NB)
                    pe.wait_ge(s.sqo, now)
                    pe.matmul(ps[:, 6, 0:H * n], m.ones[:], sqo[:].rearrange("p h n -> p (h n)"), start=True, stop=True).then_inc(s.osum, 1)
                    if not sample:
                        rwkv_p(1)
                        rwkv_dz(1)
                        rwkv_y(1)
                    pe.wait_ge(s.yc, 2 * t + 1)
                    pe.wait_ge(s.z, 2 * t + (NB if sample else 2))
                    pe.matmul(ps[:, 2, 0:2 * n], m.blk64[:], ac[:].rearrange("p c n -> p (c n)"), start=True, stop=True).then_inc(s.ymu, 1)
                    pe.wait_ge(s.bon, now)
                    pe.matmul(ps[:, 1, 0:2 * n], m.blk64[:], rk[:].rearrange("p c n -> p (c n)"), start=True, stop=True).then_inc(s.xq, 1)
                    pe.wait_ge(s.sqy, now)
                    pe.matmul(ps[:, 3, 0:2 * n], m.blk64[:], e2[:].rearrange("p c n -> p (c n)"), start=True, stop=True).then_inc(s.yvar, 1)

                loop(pe, body)
                if not sample:
                    for j in range(2):
                        last = pe.transpose(ps[:, 0, j * P:j * P + P], Z[:, 0, j, :], m.ident[:])
                else:
                    pe.wait_ge(s.z, 2 * NT + NB)
                    pe.wait_ge(s.odone, NT + 1)
                    for b in range(NB):
                        for j in range(2):
                            q = 2 * b + j
                            last = pe.transpose(ps[:, 4 + q // 4, (q % 4) * P:(q % 4) * P + P], Z[:, b, j, :], m.ident[:])
                last.then_inc(s.st_T, 1)

            @block.scalar
            def _(act):
                def body(t, c):
                    now = t + 1
                    flat = lambda a: a.rearrange("p h n -> p (h n)")
                    act.wait_ge(s.aex, now)
                    act.activation(e2[:], ac[:], ACT.Exp, scale=-DECAY)
                    act.drain()
                    act.activation(ac[:], ac[:], ACT.Exp, scale=DECAY)
                    act.activation(ax[:], ax[:], ACT.Exp, scale=DECAY).then_inc(s.e123, 1)
                    act.wait_ge(s.rows, now)
                    act.activation(flat(erow[:]), ps[:, 5, 0:H * n], ACT.Exp).then_inc(s.erow, 1)
                    act.wait_ge(s.tokT, now)
                    act.activation(tokKB[:].rearrange("p a b n -> p (a b n)"), ps[0:n, 0, :], ACT.Copy)
                    act.activation(tokV[:].rearrange("p a n -> p (a n)"), ps[0:n, 1, 0:256], ACT.Copy).then_inc(s.tokc, 1)
                    act.wait_ge(s.dtp, now)
                    act.activation(DT, DT, ACT.Exp).then_inc(s.dexp, 1)
                    for k in range(1, max(LA, LC)):
                        if k < LC - 1:
                            act.wait_ge(s.TTC, (MC - 1) * t + k)
                            act.activation(TC[:], bank(2), ACT.Copy).then_inc(s.TC, 1)
                        if k < LA - 1:
                            act.wait_ge(s.TTA, (MA - 1) * t + k)
                            act.activation(TA[:], bank(0), ACT.Copy).then_inc(s.TA, 1)

                    def pneg(cc):
                        r = slice(cs * cc, cs * cc + cs)
                        act.wait_ge(s.pp, 2 * t + cc + 1)
                        act.activation(PC[r].rearrange("p c n -> p (c n)"), ps[r, 3, 0:256], ACT.Copy, scale=-1.0).then_inc(s.pc, 1)

                    act.wait_ge(s.vn, now)
                    act.activation(vnew[:], bank(7, cols=P), ACT.Copy).then_inc(s.vnew, 1)
                    pneg(0)
                    act.wait_ge(s.o, now)
                    act.activation(sqo[:], bank(4, rows=P), ACT.Square).then_inc(s.sqo, 1)
                    act.wait_ge(s.osum, now)
                    act.activation(flat(rsA[:]), ps[:, 6, 0:H * n], ACT.Ln, scale=1.0 / HA, bias=NORM_EPS)
                    act.drain()
                    act.activation(rsA[:], rsA[:], ACT.Exp, scale=-0.5).then_inc(s.ors, 1)
                    if not sample:
                        pneg(1)
                    act.wait_ge(s.y1, 2 * t + ncs)
                    act.activation(ac[:].rearrange("p c n -> p (c n)"), ps[:, 3, 256:256 + 2 * n], ACT.Copy).then_inc(s.yc, 1)
                    act.wait_ge(s.yrs, now)
                    act.activation(e2[:], ax[:], ACT.Square).then_inc(s.sqy, 1)
                    act.wait_ge(s.yvar, now)
                    act.activation(e2[:].rearrange("p c n -> p (c n)"), ps[:, 3, 0:2 * n], ACT.Ln, scale=1.0 / HC, bias=GN_EPS)
                    act.drain()
                    act.activation(e2[:], e2[:], ACT.Exp, scale=-0.5).then_inc(s.yc, 1)

                loop(act, body)

            @block.vector
            def _(dve):
                if not sample:
                    dve.sem_inc(s.Sup, 1)
                else:
                    dve.wait_ge(s.st_T, 1)
                    dve.tensor_copy(Z[:].rearrange("p b c v -> p (b c v)"), ps[:, 4:8, :].rearrange("p a n -> p (a n)"))
                    dve.drain()
                    dve.sem_inc(s.fin, 1)

                def body(t, c):
                    now = t + 1
                    ones = m.ones[0:n, 0:n]
                    for j in range(2):
                        last = dve.tensor_tensor_scan(ac[:, j, :], reset[:], g.lw[:, j, c], 0.0, ALU.mult, ALU.add)
                    last.then_inc(s.scan, 1)
                    dve.tensor_tensor(gub[:, 0], bc(causal[0:n, 0:n], 1, H), bc(gate(g.g_all, t), 2, n), ALU.mult)
                    dve.tensor_tensor(gub[:, 1], bc(m.ident[0:n, 0:n], 1, H), bc(gate(g.beta_all, t), 2, n), ALU.mult).then_inc(s.gub, 1)
                    dve.wait_ge(s.gramK, now)

                    def mask_pairs(dst, b0, last_sem):
                        for q in range(2):
                            src = ps[0:n, b0 + q, 0:4 * n].rearrange("p (h x) -> p h x", h=2)
                            last = dve.tensor_tensor(dst[:].rearrange("p (c x) a n -> p x c (a n)", x=2)[:, q], src,
                                                     bc(rwm[0:n].rearrange("p a n -> p (a n)"), 1, 2), ALU.mult)
                        last.then_inc(last_sem, 1)

                    mask_pairs(MR, 2, s.evK)
                    dve.wait_ge(s.kvT, now)
                    dve.tensor_tensor(kbT[:], g.qkv[:, 4:8, c], rows_of(4, P), ALU.mult)
                    dve.tensor_tensor(vb[:], bank(7, cols=P), bc(gate(g.beta_all, t), 2, P), ALU.mult)
                    dve.tensor_tensor(kdec[:], bank(6, cols=P), bc(gate(g.kdf, t), 2, P), ALU.mult).then_inc(s.kbt, 1)
                    dve.wait_ge(s.erow, now)
                    for h in range(H):
                        last = dve.tensor_scalar(DT[:, h, :], rows_of(5, n)[:, h, :], gate1(g.gcum, t, h), 0.0, ALU.subtract, ALU.min)
                    last.then_inc(s.dtp, 1)
                    dve.wait_ge(s.gramB, now)
                    mask_pairs(LB, 0, s.ltC)
                    dve.wait_ge(s.dexp, now)
                    dve.tensor_tensor(DT, DT, bc(causal[0:n, 0:n], 1, H), ALU.mult)
                    dve.drain()
                    dve.wait_ge(s.gram, now)
                    dve.tensor_tensor(LTA, bank(4), DT, ALU.mult).then_inc(s.ltA, 1)
                    dve.tensor_tensor(atT[:], bank(5), DT, ALU.mult)
                    eye = bc(m.ident[0:n, 0:n], 1, H)
                    dve.wait_ge(s.c0TC, now)
                    dve.tensor_tensor(TC[:], eye, bank(2), ALU.subtract).then_inc(s.t1C, 1)
                    dve.wait_ge(s.c0TA, now)
                    dve.tensor_tensor(TA[:], eye, bank(0), ALU.subtract).then_inc(s.t1A, 1)
                    for k in range(1, max(LA, LC)):
                        if k < LC:
                            dve.wait_ge(s.YC, (MC - 1) * t + k)
                            dve.tensor_tensor(VC[:], eye, bank(2), ALU.subtract).then_inc(s.VC, 1)
                        if k < LA:
                            dve.wait_ge(s.YA, (MA - 1) * t + k)
                            dve.tensor_tensor(VA[:], eye, bank(0), ALU.subtract).then_inc(s.VA, 1)
                        if k < LC:
                            dve.wait_ge(s.TTC, (MC - 1) * t + k)
                            dve.tensor_copy(TTC[:], bank(3)).then_inc(s.TtC, 1)
                        if k < LA:
                            dve.wait_ge(s.TTA, (MA - 1) * t + k)
                            dve.tensor_copy(TTA[:], bank(1)).then_inc(s.TtA, 1)

                    def xcopy(cc):
                        r = slice(cs * cc, cs * cc + cs)
                        dve.wait_ge(s.xq, 3 * t + cc + 1)
                        dve.tensor_copy(XC[r].rearrange("p c n -> p (c n)"), ps[r, 2, 0:256]).then_inc(s.xc, 1)

                    def zup(dst, src, bnk, e):
                        for hp in range(2):
                            r = slice(64 * hp, 64 * hp + 64)
                            inc = ps[r, bnk, 256:512].rearrange("p (c x) -> p c x", c=2)[:, :, 64 * hp:64 * hp + 64]
                            dve.tensor_tensor(ztmp[r], src[r, :, r], inc, ALU.add)
                        dve.drain()
                        for hp in range(2):
                            r = slice(64 * hp, 64 * hp + 64)
                            last = dve.tensor_tensor(dst[r, :, r], ztmp[r], bc(e[r], 2, HC), ALU.mult)
                        last.then_inc(s.z, 1)

                    dve.drain()
                    dve.wait_ge(s.ks, now)
                    dve.tensor_tensor(XA[:], vb[:], bank(6, cols=P), ALU.subtract).then_inc(s.X, 1)
                    xcopy(0)
                    if not sample:
                        dve.wait_ge(s.dS, now)
                        for h in range(H):
                            last = dve.scalar_tensor_tensor(S[:, h, :], S[:, h, :],
                                                            g.gl_all[:, ds(t, 1), h:h + 1].rearrange("p o h -> p (o h)"),
                                                            bank(5, rows=P)[:, h, :], ALU.mult, ALU.add)
                        last.then_inc(s.Sup, 1)
                        dve.drain()
                        dve.wait_ge(s.dz, 2 * t + 1)
                        zup(Z[:, 1], Z[:, 0], 2, el[:, :, 0])
                        xcopy(1)
                    else:
                        for b in range(NB):
                            dve.wait_ge(s.dS, t + b + 1)
                            for h in range(H):
                                last = dve.scalar_tensor_tensor(S[b][:, h, :], S[b][:, h, :], g.glS[:, b, h:h + 1],
                                                                ps[:, (5, 7)[b % 2], h * P:h * P + P], ALU.mult, ALU.add)
                            last.then_inc(s.Sup, 1)
                        dve.wait_ge(s.y1, 2 * t + 1)
                        for b in range(NB):
                            dve.wait_ge(s.dz, 2 * t + b + 1)
                            zup(Z[:, b], Z[:, b], (2, 6)[b % 2], el[:, :, b])
                            dve.drain()
                    for j in range(2):
                        last = dve.scalar_tensor_tensor(rk[:, j, :], g.cb[:, j, c], g.vec("rwkv_r_k", j), g.cb[:, 2 + j, c], ALU.mult, ALU.mult)
                    last.then_inc(s.bon, 1)
                    dve.wait_ge(s.ors, now)
                    dve.tensor_tensor(t1[:], bank(4, rows=P), g.zg[:, :, c], ALU.mult)
                    dve.drain()
                    dve.scalar_tensor_tensor(g.zg[:, :, c], rsA[:], g.vec("gdn_norm_w"), t1[:], ALU.mult, ALU.mult).then_inc(s.odone, 1)
                    if not sample:
                        dve.drain()
                        dve.wait_ge(s.dz, 2 * t + 2)
                        dve.wait_ge(s.y1, 2 * t + 2)
                        zup(Z[:, 0], Z[:, 1], 2, el[:, :, 1])
                    two = lambda a: a.rearrange("p (c n) -> p c n", c=2)
                    dve.wait_ge(s.ymu, now)
                    dve.scalar_tensor_tensor(ax[:], two(ps[:, 2, 0:2 * n]), -1.0 / HC, ac[:], ALU.mult, ALU.add).then_inc(s.yrs, 1)
                    dve.wait_ge(s.xq, 3 * t + ncs + 1)
                    dve.tensor_tensor(rk[:], two(ps[:, 1, 0:2 * n]), g.cb[:, 4:6, c], ALU.mult)
                    dve.drain()
                    dve.wait_ge(s.yc, 2 * now)
                    dve.tensor_tensor(ax[:], ax[:], e2[:], ALU.mult)
                    dve.drain()
                    for j in range(2):
                        dve.tensor_scalar(ax[:, j, :], ax[:, j, :], g.vec("rwkv_ln_w", j), g.vec("rwkv_ln_b", j), ALU.mult, ALU.add)
                    dve.drain()
                    dve.tensor_tensor(ax[:], ax[:], rk[:], ALU.add)
                    dve.drain()
                    dve.tensor_tensor(g.cb[:, 6:8, c], g.cb[:, 6:8, c], ax[:], ALU.mult)

                loop(dve, body)
                dve.drain()
                if not sample:
                    dve.wait_ge(s.st_T, 1)
                    dve.tensor_copy(zin[:].rearrange("p a n -> p (a n)"), ps[:, 0, 0:256]).then_inc(s.outp, 1)
                else:
                    dve.wait_ge(s.st_T, 2)
                    dve.tensor_copy(zin[:].rearrange("v b c k -> v (b c k)"), ps[:, 4:8, :].rearrange("p a n -> p (a n)")).then_inc(s.outp, 1)

            @block.sync
            def _(sp):
                if sample:
                    for b in range(NB):
                        sp.dma_start(S[b], A["state_gdn"][0, b].rearrange("h k v -> k h v")).then_inc(s.outp, 16)
                    sp.wait_ge(s.ld, 1)
                    for x_ in range(2):
                        r = slice(64 * x_, 64 * x_ + 64)
                        for j in range(2):
                            sp.dma_start(zin[r, :, j, r], A["state_rwkv"][0, :, 2 * j + x_].rearrange("b v k -> v b k")).then_inc(s.outp, 16)
                    sp.wait_ge(s.outp, 16 * (NB + 4) + 1)
                    for b in range(NB):
                        sp.dma_start(O["gdn_sample"][0, b].rearrange("h k v -> k h v"), S[b]).then_inc(s.ld, 16)
                    for x_ in range(2):
                        r = slice(64 * x_, 64 * x_ + 64)
                        for j in range(2):
                            sp.dma_start(O["rwkv_sample"][0, :, 2 * j + x_].rearrange("b v k -> v b k"), zin[r, :, j, r]).then_inc(s.ld, 16)
                else:
                    sp.wait_ge(s.outp, 1)
                    sp.dma_start(O["gdn_prompt"][0, 0].rearrange("h k v -> k h v"), S[:]).then_inc(s.ld, 16)
                    for x_ in range(2):
                        r = slice(64 * x_, 64 * x_ + 64)
                        sp.dma_start(O["rwkv_prompt"][0, 0].rearrange("(c x) v k -> x v c k", x=2)[x_], zin[r, :, r]).then_inc(s.ld, 16)
                sp.wait_ge(s.ld, 16 * (NB + 4 if sample else 3) + 1)


def out_projection(nc, A, s, ps, m, g, h2T, xy, route, h2_rows):
    flat = g.qkv[:].rearrange("p a n -> p (a n)")
    wo = flat[:, 0:KD * D].rearrange("p (k d) -> p k d", k=KD)
    mt = [flat[:, (8 + u) * D:(9 + u) * D].rearrange("p (k n) -> p k n", k=KD) for u in range(2)]
    h2 = [flat[:, (10 + u) * D:(11 + u) * D] for u in range(2)]
    with ExitStack() as st:
        T = Ctx(nc, st)
        ssq = [T.sb(f"ffn_ssq_{u}", P, 2) for u in range(2)]
        wr = T.sb("w_router", P, KD, NG + NE)
        rb = T.sb("router_bias", P, NG + NE)
        L = T.sb("logits", P, TILES, NG + NE)
        pri = T.sb("first_priority", P, NG)
        mx, gmx, den, w1, w2 = (T.sb(k, P, TILES, 1) for k in ("r_max", "r_gmax", "r_den", "r_w1", "r_w2"))
        eq, oh, oh1, oh2, els, ex = (T.sb(k, P, TILES, NG) for k in ("r_eq", "r_group", "r_first", "r_second", "r_el", "r_exp"))
        tmp = T.sb("r_tmp", P, TILES, NG, EPG)
        junk = T.sb("square_junk", P, D)
        valid = T.sb("valid_sample_row", P, 1)
        strict = T.sb("strictly_before", P, P)
        iota = T.sb("iota_row", P, P)
        sel = T.sb("choice_onehot", P, 2, TILES, NE)
        sel2 = T.sb("choice_product", P, 2, TILES, NE)
        sels = T.sb("chosen", P, TILES, NE)
        rank = T.sb("rank", P, TILES, NE)
        cnt, ntile, incl, first = (T.sb(k, P, NE) for k in ("r_count", "r_ntile", "r_incl", "r_firsttile"))
        rk, fk, sk = (T.sb(k, P, 2, TILES) for k in ("r_rank", "r_choice_first", "r_slot"))
        ids = T.sb("token_ids", P, TILES)
        Arow = g.cb[:, 0:3, :].rearrange("p a n -> p (a n)")[:, 0:2 * TILES * P].rearrange("p (q n) -> p q n", n=P)
        Bcol = T.sb("slot_of_choice", P, 2, TILES, SLOTS + 1)
        lgs = g.zg[0:NG + NE, 0, :]
        with nc.Block() as block:
            def over_tiles(eng, body):
                with eng.Fori(0, NT // 2) as i:
                    for u in range(2):
                        body(2 * i + u, u, P, ds((2 * i + u) * P, P))
                body(NT, 0, NS, slice(SEQ, NTOK))

            def x_tile(t, n):
                return xy[0:n, NT, :] if n == NS else xy[:, ds(t, 1), :].rearrange("p o d -> p (o d)")

            @block.sync
            def _(sp):
                sp.dma_start(wo, A["w_out"][0].rearrange("(k p) d -> p k d", p=P)).then_inc(s.w, 16)
                sp.dma_start(xy[:, 0:NT, :], A["x_prompt"][0].rearrange("(t p) d -> p t d", p=P)).then_inc(s.x, 16)
                sp.dma_start(xy[0:NS, NT, :], A["x_sample"].rearrange("b t d -> (b t) d")).then_inc(s.x, 16)
                sp.dma_start(wr[:, :, 0:NG], A["router_group_w"][0].rearrange("(k p) c -> p k c", p=P)).then_inc(s.wr, 16)
                sp.dma_start(wr[:, :, NG:NG + NE], A["router_expert_w"][0].rearrange("(k p) c -> p k c", p=P)).then_inc(s.wr, 16)
                sp.dma_start(rb[:, 0:NG], A["router_group_b"][0].partition_broadcast(P)).then_inc(s.wr, 16)
                sp.dma_start(rb[:, NG:NG + NE], A["router_expert_b"][0].partition_broadcast(P)).then_inc(s.wr, 16)
                sp.sem_inc(s.sent, 2)

                def body(t, u, n, c):
                    sp.wait_ge(s.h2, t + 3)
                    sp.dma_start(h2_rows[c, :], h2[u][0:n, :]).then_inc(s.h2o, 16)
                    sp.wait_ge(s.h2o, 16 * (t + 1))
                    sp.sem_inc(s.sent, 1)

                over_tiles(sp, body)

            @block.gpsimd
            def _(pool):
                pool.sem_inc(s.mixT, 2)

                def body(t, u, n, c):
                    pool.wait_ge(s.out, t + 1)
                    pool.tensor_copy(mt[u][:, 0:4, 0:n], g.zg[:, :, c])
                    pool.tensor_copy(mt[u][:, 4:6, 0:n], g.ub[:, :, c])
                    pool.tensor_copy(mt[u][:, 6:8, 0:n], g.cb[:, 6:8, c]).then_inc(s.mixT, 1)

                over_tiles(pool, body)

            @block.tensor
            def _(pe):
                pe.sem_inc(s.out, 2)
                pe.wait_ge(s.w, 16)

                def body(t, u, n, c):
                    pe.wait_ge(s.mixT, t + 3)
                    pe.wait_ge(s.x2, t + 1)
                    for half in range(2):
                        for k in range(KD):
                            last = pe.matmul(ps[0:n, 2 * u + half, :], mt[u][:, k, 0:n], wo[:, k, half * 512:half * 512 + 512],
                                             start=(k == 0), stop=(k == KD - 1))
                    last.then_inc(s.out, 1)
                    pe.wait_ge(s.h2, t + 3)
                    pe.wait_ge(s.h2T, t + 1)
                    for k in range(KD):
                        last = pe.transpose(ps[:, 4 + 2 * u + k // 4, (k % 4) * P:(k % 4) * P + n], h2[u][0:n, k * P:k * P + P], m.ident[0:n, 0:n])
                    last.then_inc(s.h2p, 1)

                over_tiles(pe, body)
                pe.wait_ge(s.wr, 16 * 4)
                pe.wait_ge(s.h2T, TILES + 2)
                for c in range(3):
                    for k in range(KD):
                        last = pe.matmul(ps[0:NG + NE, c, 0:CH], wr[:, k, :], h2T[k][:, c * CH:c * CH + CH],
                                         start=(k == 0), stop=(k == KD - 1))
                last.then_inc(s.lg, 1)
                pe.wait_ge(s.lgs, 1)
                for t in range(TILES):
                    n = P if t < NT else NS
                    last = pe.transpose(ps[0:n, 4, t * (NG + NE):(t + 1) * (NG + NE)], lgs[:, tokens(t):tokens(t) + n],
                                        m.ident[0:NG + NE, 0:NG + NE])
                last.then_inc(s.lg, 1)
                pe.wait_ge(s.rt, 3)
                cols = sels[:].rearrange("p t e -> p (t e)")
                pe.matmul(ps[:, 5, 0:TILES * NE], strict[:], cols, start=True, stop=True)
                pe.matmul(ps[:, 5, TILES * NE:2 * TILES * NE], m.ones[:], cols, start=True, stop=True)
                pe.matmul(ps[:, 5, 2 * TILES * NE:2 * TILES * NE + 1], strict[:], m.ones[:, 0:1], start=True, stop=True).then_inc(s.lg, 1)
                pe.wait_ge(s.rt, 4)
                for q in range(2 * TILES):
                    last = pe.matmul(ps[:, 6, 0:SLOTS + 1], Arow[:, q, :], Bcol[:].rearrange("p c t n -> p (c t) n")[:, q, :],
                                     start=(q == 0), stop=(q == 2 * TILES - 1))
                last.then_inc(s.lg, 1)

            @block.scalar
            def _(act):
                act.preload_act_table_set(LNEXP)

                def body(t, u, n, c):
                    act.wait_ge(s.x2, t + 3)
                    act.wait_ge(s.h2, t + 1)
                    act.activation(junk[0:n, :], x_tile(t, n), ACT.Square, accum_out=ssq[u][0:n, 0:1])
                    act.drain()
                    act.activation(ssq[u][0:n, 1:2], ssq[u][0:n, 0:1], ACT.Ln, scale=1.0 / D, bias=NORM_EPS)
                    act.drain()
                    act.activation(ssq[u][0:n, 0:1], ssq[u][0:n, 1:2], ACT.Exp, scale=-0.5).then_inc(s.rstd, 1)

                over_tiles(act, body)
                act.wait_ge(s.lg, 1)
                act.activation(lgs.rearrange("p (a n) -> p a n", n=CH), ps[0:NG + NE, 0:3, 0:CH], ACT.Copy).then_inc(s.lgs, 1)
                act.wait_ge(s.rt, 1)
                act.activation(ex[:], ex[:], ACT.Exp).then_inc(s.ex, 1)
                act.wait_ge(s.rt, 2)
                act.activation(w2[:], w2[:], ACT.Exp).then_inc(s.ex, 1)

            @block.vector
            def _(dve):
                dve.sem_inc(s.x2, 2)
                dve.sem_inc(s.h2, 2)
                dve.sem_inc(s.h2T, 2)
                dve.sem_inc(s.h2p, 2)
                for i in range(NG):
                    dve.memset(pri[:, i:i + 1], float(NG - i))
                dve.memset(valid[:], 0.0)
                dve.tensor_tensor(strict[:], m.causal[:], m.ident[:], ALU.subtract)
                dve.tensor_tensor_scan(iota[:], m.ones[:], m.ones[:], 0.0, ALU.mult, ALU.add)
                dve.drain()
                dve.memset(valid[0:NS], 1.0)
                dve.tensor_scalar(iota[:], iota[:], -1.0, None, ALU.add)
                dve.wait_ge(s.x, 32)

                def body(t, u, n, c):
                    dve.wait_ge(s.out, t + 3)
                    x = x_tile(t, n)
                    dve.tensor_tensor(x, x, ps[0:n, 2 * u:2 * u + 2, :].rearrange("p a d -> p (a d)"), ALU.add).then_inc(s.x2, 1)
                    dve.wait_ge(s.rstd, t + 1)
                    dve.wait_ge(s.h2p, t + 1)
                    dve.wait_ge(s.sent, t + 1)
                    dve.tensor_scalar(h2[u][0:n, :], x, ssq[u][0:n, 0:1], None, ALU.mult).then_inc(s.h2, 1)
                    dve.wait_ge(s.h2p, t + 3)
                    src = ps[:, 4 + 2 * u:6 + 2 * u, :].rearrange("p a (k n) -> p (a k) n", n=P)
                    for i, dst in enumerate((g.ub, g.lw, g.bb)):
                        dve.tensor_tensor(dst[:, :, c], src[:, 2 * i:2 * i + 2, 0:n], bc(g.vec("norm_ffn", 2 * i, 2), 2, n), ALU.mult)
                    for i in range(2):
                        last = dve.tensor_scalar(g.kk[i][:, c], src[:, 6 + i, 0:n], g.vec("norm_ffn", 6 + i), None, ALU.mult)
                    last.then_inc(s.h2T, 1)

                over_tiles(dve, body)
                dve.memset(L[:, NT, :], 0.0)
                dve.drain()
                dve.wait_ge(s.lg, 2)
                W = NG + NE

                def step(f, *a):
                    r = f(*a)
                    dve.drain()
                    return r

                step(dve.tensor_tensor, L[:, 0:NT, :], ps[:, 4, 0:NT * W].rearrange("p (t c) -> p t c", c=W), bc(rb[:], 1, NT), ALU.add)
                step(dve.tensor_tensor, L[0:NS, NT, :], ps[0:NS, 4, NT * W:TILES * W], rb[0:NS], ALU.add)
                rep4 = lambda a: a[:].to_broadcast([P, TILES, NG])
                gl = L[:, :, 0:NG]
                el = L[:, :, NG:W].rearrange("p t (g e) -> p t g e", e=EPG)

                def first_max(vals, mval, onehot):
                    step(dve.tensor_reduce, mval[:], vals, AX_X, ALU.max)
                    step(dve.tensor_tensor, eq[:], vals, rep4(mval), ALU.is_equal)
                    step(dve.tensor_tensor, eq[:], eq[:], bc(pri[:], 1, TILES), ALU.mult)
                    step(dve.tensor_reduce, mx[:], eq[:], AX_X, ALU.max)
                    step(dve.tensor_tensor, onehot[:], eq[:], rep4(mx), ALU.is_equal)

                first_max(gl, gmx, oh)
                dve.tensor_tensor(ex[:], gl, rep4(gmx), ALU.subtract).then_inc(s.rt, 1)
                step(dve.tensor_tensor, tmp[:], el, bc(oh[:], 3, EPG), ALU.mult)
                step(dve.tensor_reduce, els[:], tmp[:].rearrange("p t g e -> p t e g"), AX_X, ALU.add)
                first_max(els[:], w1, oh1)
                step(dve.tensor_scalar, eq[:], oh1[:], -3e38, None, ALU.mult)
                step(dve.tensor_tensor, els[:], els[:], eq[:], ALU.add)
                first_max(els[:], w2, oh2)
                step(dve.tensor_tensor, w2[:], w2[:], w1[:], ALU.subtract)
                dve.sem_inc(s.rt, 1)
                dve.wait_ge(s.ex, 2)
                step(dve.tensor_reduce, den[:], ex[:], AX_X, ALU.add)
                step(dve.tensor_scalar, w1[:], w2[:], 1.0, None, ALU.add)
                step(dve.tensor_tensor, den[:], den[:], w1[:], ALU.mult)
                step(dve.reciprocal, w1[:], den[:])
                step(dve.tensor_tensor, w2[:], w2[:], w1[:], ALU.mult)
                for c, w in enumerate((w1, w2)):
                    dve.tensor_copy(route.w[:, c, :], w[:].rearrange("p t o -> p (t o)"))
                step(dve.tensor_scalar, oh[:, NT, :], oh[:, NT, :], valid[:], None, ALU.mult)
                for c, o in enumerate((oh1, oh2)):
                    dve.tensor_tensor(sel[:, c].rearrange("p t (g e) -> p t g e", e=EPG), bc(oh[:], 3, EPG), bc(o[:], 2, NG), ALU.mult)
                dve.drain()
                dve.tensor_tensor(sels[:], sel[:, 0], sel[:, 1], ALU.add).then_inc(s.rt, 1)
                dve.wait_ge(s.lg, 3)
                before = ps[:, 5, 0:TILES * NE].rearrange("p (t e) -> p t e", e=NE)
                total = ps[:, 5, TILES * NE:2 * TILES * NE].rearrange("p (t e) -> p t e", e=NE)
                step(dve.memset, cnt[:], 0.0)
                for t in range(TILES):
                    dve.tensor_tensor(rank[:, t], before[:, t], cnt[:], ALU.add)
                    dve.drain()
                    step(dve.tensor_tensor, cnt[:], cnt[:], total[:, t], ALU.add)
                step(dve.memset, ntile[:], 1.0)
                for k in range(1, TILES):
                    step(dve.scalar_tensor_tensor, ntile[:], cnt[:], k * P + 0.5, ntile[:], ALU.is_ge, ALU.add)
                step(dve.tensor_tensor_scan, incl[:], m.ones[:, 0:NE], ntile[:], 0.0, ALU.mult, ALU.add)
                step(dve.tensor_tensor, first[:], incl[:], ntile[:], ALU.subtract)
                dve.tensor_copy(route.first[:, 0:NE], first[:])
                dve.tensor_copy(route.first[:, NE:NE + 1], incl[:, NE - 1:NE])
                step(dve.tensor_tensor, sel2[:], sel[:], bc(rank[:], 1, 2), ALU.mult)
                step(dve.tensor_reduce, rk[:], sel2[:], AX_X, ALU.add)
                step(dve.tensor_tensor, sel2[:].rearrange("p c t e -> p (c t) e"), sel[:].rearrange("p c t e -> p (c t) e"),
                     bc(first[:], 1, 2 * TILES), ALU.mult)
                step(dve.tensor_reduce, fk[:], sel2[:], AX_X, ALU.add)
                step(dve.tensor_copy, sk[:], fk[:])
                for k in range(1, TILES):
                    step(dve.scalar_tensor_tensor, sk[:], rk[:], k * P - 0.5, sk[:], ALU.is_ge, ALU.add)
                step(dve.tensor_tensor, fk[:], sk[:], fk[:], ALU.subtract)
                step(dve.scalar_tensor_tensor, rk[:], fk[:], -float(P), rk[:], ALU.mult, ALU.add)
                step(dve.scalar_tensor_tensor, fk[:], sk[:], float(P), rk[:], ALU.mult, ALU.add)
                dve.tensor_copy(route.slot[:], fk[:])
                for t in range(TILES):
                    dve.tensor_scalar(ids[:, t:t + 1], ps[:, 5, 2 * TILES * NE:2 * TILES * NE + 1], float(t * P), None, ALU.add)
                dve.drain()
                step(dve.tensor_scalar, ids[:, NT:TILES], ids[:, NT:TILES], valid[:], None, ALU.mult)
                flat2 = lambda a: a[:].rearrange("p c t -> p (c t)")
                step(dve.tensor_tensor, Arow, bc(iota[:], 1, 2 * TILES), bc(flat2(rk), 2, P), ALU.is_equal)
                step(dve.tensor_tensor, Bcol[:].rearrange("p c t n -> p (c t) n"), bc(iota[:, 0:SLOTS + 1], 1, 2 * TILES),
                     bc(flat2(sk), 2, SLOTS + 1), ALU.is_equal)
                for c in range(2):
                    last = dve.tensor_tensor(Bcol[:, c], Bcol[:, c], bc(ids[:], 2, SLOTS + 1), ALU.mult)
                last.then_inc(s.rt, 1)
                dve.wait_ge(s.lg, 4)
                dve.tensor_copy(route.token[:], ps[:, 6, 0:SLOTS + 1])


def experts(nc, A, s, ps, m, g, route, h2_rows, y_rows):
    with ExitStack() as st:
        T = Ctx(nc, st)
        xg = T.sb("gathered_rows", P, D)
        idx = T.sb("gather_tokens", P, 1, dt=U32)
        zeros = T.sb("zero_rows", P, D)
        xT = T.sb("gathered_T", P, KD, P)
        he = T.sb("expert_hidden", P, FF // P, P)
        sl = [T.sb(f"silu_{u}", P, P) for u in range(2)]
        y = T.sb("expert_out", P, 2, FF)
        flat = g.qkv[:].rearrange("p a n -> p (a n)")
        cbf, zgf = g.cb[:].rearrange("p a n -> p (a n)"), g.zg[:].rearrange("p a n -> p (a n)")
        wgu = [b[:, 0:2 * KD * FF].rearrange("p (x k f) -> p x k f", x=2, k=KD) for b in (flat, cbf)]
        wd = [b.rearrange("p (k d) -> p k d", d=D) for b in (flat[:, 2 * KD * FF:2 * KD * FF + FF * KD], zgf[:, 0:FF * KD])]
        NF = FF // P
        w_in = (s.w0, s.w1)
        with nc.Block() as block:
            def over_experts(eng, slot, done):
                with eng.Fori(0, NE // 2) as i:
                    for u in range(2):
                        q0, q1 = bound(eng, 2 * i + u), bound(eng, 2 * i + u + 1)
                        with eng.Fori(q0, q1) as q:
                            slot(q, u, i)
                        done()

            def bound(eng, e):
                at = ds(e, 1) if not isinstance(e, int) else slice(e, e + 1)
                return eng.value_load(route.first[0:1, at], min_val=0, max_val=SLOTS)

            @block.sync
            def _(sp):
                with sp.Fori(0, NE // 2) as i:
                    for u in range(2):
                        e = 2 * i + u
                        sp.wait_ge(s.done, e + 1)
                        for x, name in enumerate(("expert_w_gate", "expert_w_up")):
                            sp.dma_start(wgu[u][:, x], A[name][0, ds(e, 1)].rearrange("o (k p) f -> p (o k) f", p=P)).then_inc(w_in[u], 16)
                        sp.dma_start(wd[u], A["expert_w_down"][0, ds(e, 1)].rearrange("o (k p) d -> p (o k) d", p=P)).then_inc(w_in[u], 16)
                used = bound(sp, NE)
                sp.wait_ge(s.zero, 1)
                with sp.Fori(0, SLOTS + 1 - used) as r:
                    sp.dma_start(y_rows[ds((SLOTS - r) * P, P), :], zeros[:]).then_inc(s.fill, 16)
                    sp.wait_ge(s.fill, 16 * (r + 1))
                    sp.sem_inc(s.filled, 1)

            @block.gpsimd
            def _(pool):
                pool.memset(zeros[:], 0.0)
                pool.drain()
                pool.sem_inc(s.zero, 1)
                with pool.Fori(0, bound(pool, NE) + 1) as q:
                    pool.wait_ge(s.xTp, q + 1)
                    pool.tensor_copy(idx[:], route.token[:, ds(q, 1)])
                    pool.drain()
                    pool.indirect_dma_start(xg[:], None, h2_rows,
                                            bass.IndirectOffsetOnAxis(ap=idx[:], axis=0)).then_inc(s.gather, 16)

            @block.tensor
            def _(pe):
                pe.sem_inc(s.xTp, 1)
                pe.sem_inc(s.done, 2)
                pe.sem_inc(s.down, 2)

                def transposes(q):
                    pe.wait_ge(s.gather, 16 * (q + 1))
                    for k in range(KD):
                        last = pe.transpose(ps[:, 6 + k // 4, (k % 4) * P:(k % 4) * P + P], xg[:, k * P:k * P + P], m.ident[:])
                    last.then_inc(s.xTp, 1)

                transposes(0)

                def slot(q, u, i):
                    pe.wait_ge(w_in[u], 48 * (i + 1))
                    pe.wait_ge(s.xT, q + 1)
                    for f in range(NF):
                        pe.wait_ge(s.he, NF * q + f + 1)
                        for x in range(2):
                            for k in range(KD):
                                last = pe.matmul(ps[:, 2 * (f % 2) + x, 0:P], wgu[u][:, x, k, f * P:f * P + P], xT[:, k, :],
                                                 start=(k == 0), stop=(k == KD - 1))
                        last.then_inc(s.gu, 1)
                    transposes(q + 1)
                    pe.wait_ge(s.he, NF * (q + 1) + 2)
                    for half in range(2):
                        pe.wait_ge(s.acc, 2 * q + half + 1)
                        for k in range(NF):
                            last = pe.matmul(ps[:, 4 + half, :], he[:, k, :], wd[u][:, k, half * 512:half * 512 + 512],
                                             start=(k == 0), stop=(k == NF - 1))
                        last.then_inc(s.down, 1)

                def done():
                    pe.drain()
                    pe.sem_inc(s.done, 1)

                over_experts(pe, slot, done)

            @block.scalar
            def _(act):
                act.sem_inc(s.acc, 2)
                with act.Fori(0, bound(act, NE)) as q:
                    for f in range(NF):
                        act.wait_ge(s.gu, NF * q + f + 1)
                        act.wait_ge(s.he, NF * q + f + 1)
                        act.activation(sl[f % 2][:], ps[:, 2 * (f % 2), 0:P], ACT.Silu).then_inc(s.silu, 1)
                    for half in range(2):
                        act.wait_ge(s.down, 2 * q + half + 3)
                        act.activation(y[:, half, :], ps[:, 4 + half, :], ACT.Copy).then_inc(s.acc, 1)
                    act.drain()
                    act.dma_start(y_rows[ds(q * P, P), :], y[:].rearrange("p a n -> p (a n)")).then_inc(s.yout, 16)
                    act.wait_ge(s.yout, 16 * (q + 1))

            @block.vector
            def _(dve):
                dve.sem_inc(s.he, 2)
                nf = g.vec("norm_ffn", 0, KD)

                def channels(q):
                    dve.wait_ge(s.xTp, q + 2)
                    dve.tensor_tensor(xT[:], ps[:, 6:8, :].rearrange("p a (k n) -> p (a k) n", n=P), bc(nf, 2, P), ALU.mult).then_inc(s.xT, 1)

                channels(0)
                with dve.Fori(0, bound(dve, NE)) as q:
                    for f in range(NF):
                        dve.wait_ge(s.silu, NF * q + f + 1)
                        dve.wait_ge(s.down, 2 * q + 2)
                        dve.tensor_tensor(he[:, f, :], sl[f % 2][:], ps[:, 2 * (f % 2) + 1, 0:P], ALU.mult).then_inc(s.he, 1)
                    channels(q + 1)


def combine(nc, A, O, s, g, xy, route, y_rows):
    with ExitStack() as st:
        T = Ctx(nc, st)
        flat = g.qkv[:].rearrange("p a n -> p (a n)")
        wrow, junk = flat[:, 0:D], flat[:, D:2 * D]
        rows = [[flat[:, (2 + 2 * b + c) * D:(3 + 2 * b + c) * D] for c in range(2)] for b in range(3)]
        got = (s.c0, s.c1, s.c2)
        ssq = T.sb("final_ssq", P, TILES, 2)
        with nc.Block() as block:
            @block.gpsimd
            def _(pool):
                for t in range(TILES):
                    n = P if t < NT else NS
                    if t >= 3:
                        pool.wait_ge(s.used, t - 2)
                    for c in range(2):
                        pool.indirect_dma_start(rows[t % 3][c][0:n], None, y_rows,
                                                bass.IndirectOffsetOnAxis(ap=route.slot[0:n, c, t:t + 1], axis=0)).then_inc(got[t % 3], 16)

            @block.sync
            def _(sp):
                sp.dma_start(wrow, A["norm_final"].partition_broadcast(P)).then_inc(s.w, 16)
                for t in range(TILES):
                    sp.wait_ge(s.y, t + 1)
                    dst = O["y_prompt"][0, t * P:t * P + P, :] if t < NT else O["y_sample"].rearrange("b t d -> (b t) d")
                    sp.dma_start(dst, xy[0:(P if t < NT else NS), t, :]).then_inc(s.out, 16)
                sp.wait_ge(s.out, 16 * TILES)

            @block.scalar
            def _(act):
                act.preload_act_table_set(LNEXP)
                for t in range(TILES):
                    n = P if t < NT else NS
                    act.drain()
                    act.wait_ge(s.used, t + 1)
                    act.activation(junk[0:n], xy[0:n, t, :], ACT.Square, accum_out=ssq[0:n, t, 0:1])
                    act.drain()
                    act.activation(ssq[0:n, t, 1:2], ssq[0:n, t, 0:1], ACT.Ln, scale=1.0 / D, bias=NORM_EPS)
                    act.drain()
                    act.activation(ssq[0:n, t, 0:1], ssq[0:n, t, 1:2], ACT.Exp, scale=-0.5).then_inc(s.rstd, 1)

            @block.vector
            def _(dve):
                def add(t):
                    n = P if t < NT else NS
                    dve.wait_ge(got[t % 3], 32 * (t // 3 + 1))
                    for c in range(2):
                        last = dve.scalar_tensor_tensor(xy[0:n, t, :], rows[t % 3][c][0:n], route.w[0:n, c, t:t + 1], xy[0:n, t, :], ALU.mult, ALU.add)
                        if c == 0:
                            dve.drain()
                    last.then_inc(s.used, 1)

                dve.wait_ge(s.w, 16)
                add(0)
                for t in range(TILES):
                    n = P if t < NT else NS
                    if t + 1 < TILES:
                        add(t + 1)
                    dve.wait_ge(s.rstd, t + 1)
                    dve.scalar_tensor_tensor(xy[0:n, t, :], xy[0:n, t, :], ssq[0:n, t, 0:1], wrow[0:n], ALU.mult, ALU.mult).then_inc(s.y, 1)


_IN_NAMES = """x_prompt x_sample state_gdn state_gdn_conv state_rwkv state_rwkv_shift norm_mix norm_ffn norm_final w_in
gdn_conv_w gdn_a_log gdn_dt_bias gdn_norm_w sgu_ln_w sgu_ln_b sgu_w sgu_b rwkv_mu rwkv_w0 rwkv_w_up rwkv_a0
rwkv_a_up rwkv_g_up rwkv_k_k rwkv_k_a rwkv_r_k rwkv_ln_w rwkv_ln_b w_out router_group_w router_group_b
router_expert_w router_expert_b expert_w_gate expert_w_up expert_w_down""".split()
_OUT_SHAPES = (
    ("y_prompt", (1, SEQ, D)),
    ("y_sample", (NB, TB, D)),
    ("gdn_prompt", (1, 1, H, HA, HA)),
    ("gdn_conv_prompt", (1, 1, CW - 1, 3 * DA)),
    ("rwkv_prompt", (1, 1, H, HC, HC)),
    ("shift_prompt", (1, 1, D)),
    ("gdn_sample", (1, NB, H, HA, HA)),
    ("gdn_conv_sample", (1, NB, CW - 1, 3 * DA)),
    ("rwkv_sample", (1, NB, H, HC, HC)),
    ("shift_sample", (1, NB, D)),
    ("chunk_v_sample", (1, NB, TB, DB)),
)


def kernel(**inputs):
    import numpy as _np
    import concourse.bacc as _bacc
    from concourse import mybir as _mybir
    from concourse.bass_utils import run_bass_kernel_spmd as _run

    nc = _bacc.Bacc("TRN2", target_bir_lowering=False, num_devices=1)
    arrays, ins, outs = {}, {}, {}
    for name, shape in _OUT_SHAPES:
        outs[name] = nc.dram_tensor(f"out_{name}", list(shape), _mybir.dt.float32, kind="ExternalOutput").ap()
    for name in _IN_NAMES:
        arrays[f"in_{name}"] = _np.ascontiguousarray(inputs[name])
        ins[name] = nc.dram_tensor(f"in_{name}", arrays[f"in_{name}"].shape, _mybir.dt.float32, kind="ExternalInput").ap()
    build(nc, ins, outs)
    r = _run(nc, [arrays], core_ids=[0])
    return tuple(r.results[0][f"out_{name}"] for name, _ in _OUT_SHAPES)
```
